# Optimizing a Trainium2 kernel written in Bass

```python
import math
import jax, jax.numpy as jnp
from jax import lax
import numpy as np

D_MODEL = 1024
BATCH = 1
SEQ = 512
DEPTH = 1

HEAD_DIM = 128
MIX_WIDTH = D_MODEL
GDN_WIDTH = MIX_WIDTH // 2
RET_WIDTH = MIX_WIDTH - GDN_WIDTH
GDN_HEADS = GDN_WIDTH // HEAD_DIM
RET_HEADS = RET_WIDTH // HEAD_DIM
SHORT_CONV = 4
FFN_CONV = 3
D_FF = ((8 * D_MODEL // 3 + 255) // 256) * 256
CHUNK = 64
RET_ROPE_BASE = 10000.0
EPS = 1e-6
IN_SPLITS = (GDN_WIDTH, GDN_WIDTH, GDN_WIDTH, GDN_WIDTH, GDN_HEADS, GDN_HEADS,
             RET_WIDTH, RET_WIDTH, RET_WIDTH, RET_WIDTH)
IN_COLS = 4 * GDN_WIDTH + 2 * GDN_HEADS + 4 * RET_WIDTH


def _rms_norm(x, w):
    xf = x.astype(jnp.float32)
    y = xf * lax.rsqrt(jnp.mean(xf * xf, axis=-1, keepdims=True) + EPS)
    return (y * w.astype(jnp.float32)).astype(x.dtype)

def _rms_f32(xf):
    return xf * lax.rsqrt(jnp.mean(xf * xf, axis=-1, keepdims=True) + EPS)

def _l2norm(xf):
    return xf * lax.rsqrt(jnp.sum(xf * xf, axis=-1, keepdims=True) + EPS)

def _causal_dwconv(x, w):
    k, c = w.shape
    return lax.conv_general_dilated(
        x, w[:, None, :].astype(x.dtype), window_strides=(1,), padding=[(k - 1, 0)],
        dimension_numbers=("NWC", "WIO", "NWC"), feature_group_count=c)

def _to_chunks(t):
    b, s, h, d = t.shape
    return t.reshape(b, s // CHUNK, CHUNK, h, d).transpose(1, 0, 3, 2, 4)

def _from_chunks(t):
    nc, b, h, c, d = t.shape
    return t.transpose(1, 0, 3, 2, 4).reshape(b, nc * c, h, d)

def _scalar_chunks(t):
    b, s, h = t.shape
    return t.reshape(b, s // CHUNK, CHUNK, h).transpose(1, 0, 3, 2)

def _gated_deltanet(q, k, v, gate, a, b, conv_w, a_log, dt_bias, norm_w):
    bsz, s, _ = q.shape
    h, d = GDN_HEADS, HEAD_DIM
    qkv = jax.nn.silu(_causal_dwconv(jnp.concatenate([q, k, v], axis=-1), conv_w))
    qkv = qkv.astype(jnp.float32)
    q, k, v = jnp.split(qkv, 3, axis=-1)
    q = _l2norm(q.reshape(bsz, s, h, d)) * (d ** -0.5)
    k = _l2norm(k.reshape(bsz, s, h, d))
    v = v.reshape(bsz, s, h, d)
    beta = jax.nn.sigmoid(b.astype(jnp.float32))
    g = -jnp.exp(a_log.astype(jnp.float32)) * jax.nn.softplus(
        a.astype(jnp.float32) + dt_bias.astype(jnp.float32))

    qc, kc, vc = _to_chunks(q), _to_chunks(k), _to_chunks(v)
    gcum = jnp.cumsum(_scalar_chunks(g), axis=-1)
    betac = _scalar_chunks(beta)
    causal = jnp.tril(jnp.ones((CHUNK, CHUNK), dtype=bool))
    strict = jnp.tril(jnp.ones((CHUNK, CHUNK), dtype=bool), -1)
    diff = gcum[..., :, None] - gcum[..., None, :]
    decay = jnp.exp(jnp.where(causal, diff, -jnp.inf))
    kb = kc * betac[..., None]
    vb = vc * betac[..., None]
    m = jnp.where(strict, jnp.einsum('nbhik,nbhjk->nbhij', kb, kc) * decay, 0.0)
    eye = jnp.eye(CHUNK, dtype=jnp.float32)
    t_mat = lax.linalg.triangular_solve(eye + m, jnp.broadcast_to(eye, m.shape),
                                        left_side=True, lower=True, unit_diagonal=True)
    u_base = jnp.einsum('nbhij,nbhjv->nbhiv', t_mat, vb)
    w_mat = jnp.einsum('nbhij,nbhjk->nbhik', t_mat, kb * jnp.exp(gcum)[..., None])
    qk = jnp.einsum('nbhik,nbhjk->nbhij', qc, kc) * decay
    q_dec = qc * jnp.exp(gcum)[..., None]
    k_dec = kc * jnp.exp(gcum[..., -1:] - gcum)[..., None]
    chunk_decay = jnp.exp(gcum[..., -1])

    def step(state, inp):
        u_b, w_c, qk_c, qd_c, kd_c, cd_c = inp
        u = u_b - jnp.einsum('bhck,bhkv->bhcv', w_c, state)
        o = jnp.einsum('bhck,bhkv->bhcv', qd_c, state) + jnp.einsum('bhij,bhjv->bhiv', qk_c, u)
        state = state * cd_c[..., None, None] + jnp.einsum('bhck,bhcv->bhkv', kd_c, u)
        return state, o

    s0 = jnp.zeros((bsz, h, d, d), dtype=jnp.float32)
    _, o = lax.scan(step, s0, (u_base, w_mat, qk, q_dec, k_dec, chunk_decay))
    o = _from_chunks(o)
    gt = gate.astype(jnp.float32).reshape(bsz, s, h, d)
    o = _rms_f32(o) * norm_w.astype(jnp.float32) * jax.nn.silu(gt)
    return o.reshape(bsz, s, h * d).astype(gate.dtype)

def _rotate_every_two(x):
    x1 = x[..., ::2]
    x2 = x[..., 1::2]
    return jnp.stack((-x2, x1), axis=-1).reshape(x.shape)

def _xpos_rotary(x, pos):
    d = x.shape[-1]
    angle = 1.0 / (RET_ROPE_BASE ** jnp.linspace(0.0, 1.0, d // 2, dtype=jnp.float32))
    angle = jnp.repeat(angle, 2)
    phase = pos[:, None] * angle[None, :]
    return x * jnp.cos(phase)[:, None, :] + _rotate_every_two(x) * jnp.sin(phase)[:, None, :]

def _retention(q, k, v, gate):
    bsz, s, _ = q.shape
    h, d = RET_HEADS, HEAD_DIM
    pos = jnp.arange(s, dtype=jnp.float32)
    q = _xpos_rotary(q.astype(jnp.float32).reshape(bsz, s, h, d), pos)
    k = _xpos_rotary(k.astype(jnp.float32).reshape(bsz, s, h, d), pos) * (d ** -0.5)
    v = v.astype(jnp.float32).reshape(bsz, s, h, d)
    log_gamma = jnp.log(1.0 - jnp.exp2(-5.0 - jnp.arange(h, dtype=jnp.float32)))
    idx = jnp.arange(CHUNK, dtype=jnp.float32)
    causal = jnp.tril(jnp.ones((CHUNK, CHUNK), dtype=bool))
    rel = idx[:, None] - idx[None, :]
    d_mat = jnp.exp(jnp.where(causal[None], rel[None] * log_gamma[:, None, None], -jnp.inf))
    xi = jnp.exp((idx[None, :] + 1.0) * log_gamma[:, None])[..., None]
    zeta = jnp.exp((CHUNK - 1.0 - idx[None, :]) * log_gamma[:, None])[..., None]
    chunk_gamma = jnp.exp(CHUNK * log_gamma)

    qc, kc, vc = _to_chunks(q), _to_chunks(k), _to_chunks(v)
    inner = jnp.einsum('nbhij,nbhjv->nbhiv',
                       jnp.einsum('nbhik,nbhjk->nbhij', qc, kc) * d_mat, vc)
    q_xi = qc * xi
    kv = jnp.einsum('nbhck,nbhcv->nbhkv', kc * zeta, vc)

    def step(r, inp):
        inner_c, qx_c, kv_c = inp
        o = inner_c + jnp.einsum('bhck,bhkv->bhcv', qx_c, r)
        r = r * chunk_gamma[:, None, None] + kv_c
        return r, o

    r0 = jnp.zeros((bsz, h, d, d), dtype=jnp.float32)
    _, o = lax.scan(step, r0, (inner, q_xi, kv))
    o = _rms_f32(_from_chunks(o))
    o = jax.nn.silu(gate.astype(jnp.float32).reshape(bsz, s, h, d)) * o
    return o.reshape(bsz, s, h * d).astype(gate.dtype)

def _conv_glu_mlp(x, w_up, conv_w, w_down):
    hdn = jnp.einsum('bsd,df->bsf', x, w_up)
    hdn = _causal_dwconv(hdn, conv_w)
    g, u = jnp.split(hdn, 2, axis=-1)
    return jnp.einsum('bsf,fd->bsd', jax.nn.silu(g) * u, w_down)

def first_inputs(seed: int = 0) -> dict:
    key = jax.random.key(seed)
    ks = jax.random.split(key, 14)
    f32 = jnp.float32
    x = jax.random.normal(ks[0], (BATCH, SEQ, D_MODEL), f32)
    attn_norm_w = 1.0 + 0.02 * jax.random.normal(ks[1], (DEPTH, D_MODEL), f32)
    w_in = jax.random.normal(ks[2], (DEPTH, D_MODEL, IN_COLS), f32) * D_MODEL ** -0.5
    gdn_conv_w = jax.random.normal(ks[3], (DEPTH, SHORT_CONV, 3 * GDN_WIDTH), f32) * SHORT_CONV ** -0.5
    gdn_a_log = jnp.log(jax.random.uniform(ks[4], (DEPTH, GDN_HEADS), f32, minval=1.0, maxval=16.0))
    dt = jnp.exp(jax.random.uniform(ks[5], (DEPTH, GDN_HEADS), f32,
                                    minval=math.log(1e-3), maxval=math.log(1e-1)))
    gdn_dt_bias = dt + jnp.log(-jnp.expm1(-dt))
    gdn_norm_w = 1.0 + 0.02 * jax.random.normal(ks[6], (DEPTH, HEAD_DIM), f32)
    w_out = jax.random.normal(ks[7], (DEPTH, MIX_WIDTH, D_MODEL), f32) * MIX_WIDTH ** -0.5
    mlp_norm_w = 1.0 + 0.02 * jax.random.normal(ks[8], (DEPTH, D_MODEL), f32)
    w_up = jax.random.normal(ks[9], (DEPTH, D_MODEL, 2 * D_FF), f32) * D_MODEL ** -0.5
    mlp_conv_w = jax.random.normal(ks[10], (DEPTH, FFN_CONV, 2 * D_FF), f32) * FFN_CONV ** -0.5
    w_down = jax.random.normal(ks[11], (DEPTH, D_FF, D_MODEL), f32) * D_FF ** -0.5
    final_norm_w = 1.0 + 0.02 * jax.random.normal(ks[12], (D_MODEL,), f32)
    return {"x": x, "attn_norm_w": attn_norm_w, "w_in": w_in, "gdn_conv_w": gdn_conv_w,
            "gdn_a_log": gdn_a_log, "gdn_dt_bias": gdn_dt_bias, "gdn_norm_w": gdn_norm_w,
            "w_out": w_out, "mlp_norm_w": mlp_norm_w, "w_up": w_up, "mlp_conv_w": mlp_conv_w,
            "w_down": w_down, "final_norm_w": final_norm_w}

def first_block(x, attn_norm_w, w_in, gdn_conv_w, gdn_a_log, gdn_dt_bias, gdn_norm_w,
              w_out, mlp_norm_w, w_up, mlp_conv_w, w_down, final_norm_w):
    split_idx = []
    acc = 0
    for sz in IN_SPLITS[:-1]:
        acc += sz
        split_idx.append(acc)
    h = x
    for l in range(DEPTH):
        n = _rms_norm(h, attn_norm_w[l])
        proj = jnp.einsum('bsd,dc->bsc', n, w_in[l])
        (gq, gk, gv, gg, ga, gb, rq, rk, rv, rg) = jnp.split(proj, split_idx, axis=-1)
        o_gdn = _gated_deltanet(gq, gk, gv, gg, ga, gb, gdn_conv_w[l], gdn_a_log[l],
                                gdn_dt_bias[l], gdn_norm_w[l])
        o_ret = _retention(rq, rk, rv, rg)
        mix = jnp.concatenate([o_gdn, o_ret], axis=-1)
        h = h + jnp.einsum('bsm,md->bsd', mix, w_out[l])
        n2 = _rms_norm(h, mlp_norm_w[l])
        h = h + _conv_glu_mlp(n2, w_up[l], mlp_conv_w[l], w_down[l])
    return _rms_norm(h, final_norm_w)


DEPTH_2 = 2

N_ATTN_HEADS = 8
HEAD_DIM_2 = D_MODEL // 16
ATTN_DIM = N_ATTN_HEADS * HEAD_DIM_2
Q_BLOCK = 128
FORGET_BIAS_MEAN = 3.0
POOL_WINDOWS = (2, 4, 8, 16)
N_POOL_GROUPS = len(POOL_WINDOWS)
POOL_GROUP_DIM = D_MODEL // 8
POOL_DIM = N_POOL_GROUPS * POOL_GROUP_DIM
EVEN_IN_DIM = 3 * ATTN_DIM + N_ATTN_HEADS + POOL_DIM
EVEN_MIX_DIM = ATTN_DIM + POOL_DIM
CONV_DIM = D_MODEL
CONV_WIDTH = 31
D_FF_2 = 2816
FFN_CONV_WIDTH = 3

N_EVEN = (DEPTH_2 + 1) // 2
N_ODD = DEPTH_2 // 2


def rms_norm(x, g):
    xf = x.astype(jnp.float32)
    y = xf * lax.rsqrt(jnp.mean(xf * xf, axis=-1, keepdims=True) + EPS)
    return (y * g.astype(jnp.float32)).astype(x.dtype)

def layer_norm(x, g, b):
    xf = x.astype(jnp.float32)
    mu = jnp.mean(xf, axis=-1, keepdims=True)
    xc = xf - mu
    y = xc * lax.rsqrt(jnp.mean(xc * xc, axis=-1, keepdims=True) + EPS)
    return (y * g.astype(jnp.float32) + b.astype(jnp.float32)).astype(x.dtype)

def causal_dwconv(x, w, b):
    k_width, ch = w.shape
    y = lax.conv_general_dilated(
        x, w[:, None, :].astype(x.dtype), window_strides=(1,), padding=[(k_width - 1, 0)],
        dimension_numbers=("NWC", "WIO", "NWC"), feature_group_count=ch)
    return y + b.astype(x.dtype)

def forgetting_attention(q, k, v, f_logit, q_g, k_g):
    bsz, seq, nh, dh = q.shape
    nb = seq // Q_BLOCK
    q = rms_norm(q, q_g)
    k = rms_norm(k, k_g)
    scale = 1.0 / math.sqrt(dh)
    c = jnp.cumsum(jax.nn.log_sigmoid(f_logit.astype(jnp.float32)), axis=1)
    c_k = jnp.transpose(c, (0, 2, 1))
    k_h = jnp.transpose(k, (0, 2, 1, 3))
    v_h = jnp.transpose(v, (0, 2, 1, 3))
    q_blocks = q.reshape(bsz, nb, Q_BLOCK, nh, dh).transpose(1, 0, 3, 2, 4)
    c_blocks = c.reshape(bsz, nb, Q_BLOCK, nh).transpose(1, 0, 3, 2)
    k_pos = jnp.arange(seq)

    def one_block(args):
        q_blk, cq_blk, blk = args
        q_pos = blk * Q_BLOCK + jnp.arange(Q_BLOCK)
        s = jnp.einsum("bhqd,bhkd->bhqk", q_blk, k_h).astype(jnp.float32) * scale
        s = s + cq_blk[..., :, None] - c_k[:, :, None, :]
        mask = k_pos[None, :] <= q_pos[:, None]
        s = jnp.where(mask[None, None], s, -jnp.inf)
        p = jax.nn.softmax(s, axis=-1)
        return jnp.einsum("bhqk,bhkd->bhqd", p.astype(v_h.dtype), v_h)

    out = lax.map(one_block, (q_blocks, c_blocks, jnp.arange(nb)))
    return out.transpose(1, 0, 3, 2, 4).reshape(bsz, seq, nh * dh)

def multiscale_pool(u, w_pool, pool_scale):
    bsz, seq, _ = u.shape
    ug = u.reshape(bsz, seq, N_POOL_GROUPS, POOL_GROUP_DIM)
    csz = jnp.pad(jnp.cumsum(ug.astype(jnp.float32), axis=1), ((0, 0), (1, 0), (0, 0), (0, 0)))
    pos = jnp.arange(1, seq + 1, dtype=jnp.float32)
    outs = []
    for g, w in enumerate(POOL_WINDOWS):
        upper = csz[:, 1:, g]
        lower = jnp.pad(csz[:, : seq + 1 - w, g], ((0, 0), (w - 1, 0), (0, 0)))
        count = jnp.minimum(pos, float(w))[None, :, None]
        outs.append((upper - lower) / count)
    pooled = jnp.stack(outs, axis=2).astype(u.dtype)
    mixed = pooled - ug
    y = jnp.einsum("bsgc,gcd->bsgd", mixed, w_pool).reshape(bsz, seq, POOL_DIM)
    return y * pool_scale

def even_mixer(h, w_in, b_f, q_g, k_g, w_pool, pool_scale, w_out):
    bsz, seq, _ = h.shape
    z = h @ w_in
    o = 0
    q = z[..., o:o + ATTN_DIM].reshape(bsz, seq, N_ATTN_HEADS, HEAD_DIM_2); o += ATTN_DIM
    k = z[..., o:o + ATTN_DIM].reshape(bsz, seq, N_ATTN_HEADS, HEAD_DIM_2); o += ATTN_DIM
    v = z[..., o:o + ATTN_DIM].reshape(bsz, seq, N_ATTN_HEADS, HEAD_DIM_2); o += ATTN_DIM
    f_logit = z[..., o:o + N_ATTN_HEADS] + b_f; o += N_ATTN_HEADS
    u = z[..., o:o + POOL_DIM]
    a_out = forgetting_attention(q, k, v, f_logit, q_g, k_g)
    p_out = multiscale_pool(u, w_pool, pool_scale)
    return jnp.concatenate([a_out, p_out], axis=-1) @ w_out

def conformer_conv(h, w_pw1, dw_w, dw_b, ln_g, ln_b, w_pw2):
    a, g = jnp.split(h @ w_pw1, 2, axis=-1)
    u = a * jax.nn.sigmoid(g)
    u = causal_dwconv(u, dw_w, dw_b)
    u = jax.nn.silu(layer_norm(u, ln_g, ln_b))
    return u @ w_pw2

def conv_ffn(h, w_up, conv_w, conv_b, w_down):
    u = causal_dwconv(h @ w_up, conv_w, conv_b)
    gate, val = jnp.split(u, 2, axis=-1)
    return (jax.nn.silu(gate) * val) @ w_down

def second_inputs(seed: int = 0) -> dict:
    key = jax.random.key(seed)
    ks = jax.random.split(key, 24)
    nrm = lambda k, shape, s: jax.random.normal(k, shape, jnp.float32) * s
    d = D_MODEL
    return {
        "x": nrm(ks[0], (BATCH, SEQ, d), 1.0),
        "even_norm_g": 1.0 + nrm(ks[1], (N_EVEN, d), 0.05),
        "even_w_in": nrm(ks[2], (N_EVEN, d, EVEN_IN_DIM), d ** -0.5),
        "even_b_f": FORGET_BIAS_MEAN + nrm(ks[3], (N_EVEN, N_ATTN_HEADS), 0.5),
        "even_q_norm_g": 1.0 + nrm(ks[4], (N_EVEN, HEAD_DIM_2), 0.05),
        "even_k_norm_g": 1.0 + nrm(ks[5], (N_EVEN, HEAD_DIM_2), 0.05),
        "even_w_pool": nrm(ks[6], (N_EVEN, N_POOL_GROUPS, POOL_GROUP_DIM, POOL_GROUP_DIM), POOL_GROUP_DIM ** -0.5),
        "even_pool_scale": 1.0 + nrm(ks[7], (N_EVEN, POOL_DIM), 0.1),
        "even_w_out": nrm(ks[8], (N_EVEN, EVEN_MIX_DIM, d), EVEN_MIX_DIM ** -0.5),
        "odd_norm_g": 1.0 + nrm(ks[9], (N_ODD, d), 0.05),
        "odd_w_pw1": nrm(ks[10], (N_ODD, d, 2 * CONV_DIM), d ** -0.5),
        "odd_dw_w": nrm(ks[11], (N_ODD, CONV_WIDTH, CONV_DIM), CONV_WIDTH ** -0.5),
        "odd_dw_b": nrm(ks[12], (N_ODD, CONV_DIM), 0.02),
        "odd_ln_g": 1.0 + nrm(ks[13], (N_ODD, CONV_DIM), 0.05),
        "odd_ln_b": nrm(ks[14], (N_ODD, CONV_DIM), 0.02),
        "odd_w_pw2": nrm(ks[15], (N_ODD, CONV_DIM, d), CONV_DIM ** -0.5),
        "ffn_norm_g": 1.0 + nrm(ks[16], (DEPTH_2, d), 0.05),
        "ffn_w_up": nrm(ks[17], (DEPTH_2, d, 2 * D_FF_2), d ** -0.5),
        "ffn_conv_w": nrm(ks[18], (DEPTH_2, FFN_CONV_WIDTH, 2 * D_FF_2), FFN_CONV_WIDTH ** -0.5),
        "ffn_conv_b": nrm(ks[19], (DEPTH_2, 2 * D_FF_2), 0.02),
        "ffn_w_down": nrm(ks[20], (DEPTH_2, D_FF_2, d), D_FF_2 ** -0.5),
    }

def second_block(x, even_norm_g, even_w_in, even_b_f, even_q_norm_g, even_k_norm_g, even_w_pool,
              even_pool_scale, even_w_out, odd_norm_g, odd_w_pw1, odd_dw_w, odd_dw_b, odd_ln_g,
              odd_ln_b, odd_w_pw2, ffn_norm_g, ffn_w_up, ffn_conv_w, ffn_conv_b, ffn_w_down):
    for layer in range(DEPTH_2):
        i = layer // 2
        if layer % 2 == 0:
            h = rms_norm(x, even_norm_g[i])
            x = x + even_mixer(h, even_w_in[i], even_b_f[i], even_q_norm_g[i], even_k_norm_g[i],
                               even_w_pool[i], even_pool_scale[i], even_w_out[i])
        else:
            h = rms_norm(x, odd_norm_g[i])
            x = x + conformer_conv(h, odd_w_pw1[i], odd_dw_w[i], odd_dw_b[i], odd_ln_g[i],
                                   odd_ln_b[i], odd_w_pw2[i])
        h = rms_norm(x, ffn_norm_g[layer])
        x = x + conv_ffn(h, ffn_w_up[layer], ffn_conv_w[layer], ffn_conv_b[layer], ffn_w_down[layer])
    return x


def setup_inputs(seed=0):
    out = dict(first_inputs(seed))
    for name, value in second_inputs(seed + 1).items():
        if name != "x":
            out[name + "_2"] = value
    return out


def reference(
    x, attn_norm_w, w_in, gdn_conv_w, gdn_a_log, gdn_dt_bias, gdn_norm_w, w_out, mlp_norm_w,
    w_up, mlp_conv_w, w_down, final_norm_w, even_norm_g_2, even_w_in_2, even_b_f_2,
    even_q_norm_g_2, even_k_norm_g_2, even_w_pool_2, even_pool_scale_2, even_w_out_2,
    odd_norm_g_2, odd_w_pw1_2, odd_dw_w_2, odd_dw_b_2, odd_ln_g_2, odd_ln_b_2, odd_w_pw2_2,
    ffn_norm_g_2, ffn_w_up_2, ffn_conv_w_2, ffn_conv_b_2, ffn_w_down_2,
):
    x = first_block(
        x, attn_norm_w, w_in, gdn_conv_w, gdn_a_log, gdn_dt_bias, gdn_norm_w, w_out, mlp_norm_w,
        w_up, mlp_conv_w, w_down, final_norm_w,
    )
    return second_block(
        x, even_norm_g_2, even_w_in_2, even_b_f_2, even_q_norm_g_2, even_k_norm_g_2,
        even_w_pool_2, even_pool_scale_2, even_w_out_2, odd_norm_g_2, odd_w_pw1_2, odd_dw_w_2,
        odd_dw_b_2, odd_ln_g_2, odd_ln_b_2, odd_w_pw2_2, ffn_norm_g_2, ffn_w_up_2, ffn_conv_w_2,
        ffn_conv_b_2, ffn_w_down_2,
    )


_drawn_inputs = setup_inputs


def setup_inputs(seed=0):
    import zlib

    import numpy as np

    out = dict(_drawn_inputs(seed))
    spreads = {}
    factors = {'gdn_norm_w': 5.494,
     'mlp_norm_w': 3.598,
     'even_q_norm_g_2': 5.637,
     'even_k_norm_g_2': 4.501,
     'odd_dw_b_2': 3.266,
     'odd_ln_b_2': 6.625,
     'ffn_conv_b_2': 3.185}
    for name, (base, spread) in spreads.items():
        noise = np.random.default_rng([zlib.crc32(name.encode()), seed]).standard_normal(out[name].shape)
        drawn = base * np.exp(spread * noise) if base else spread * noise
        out[name] = __import__('jax').numpy.asarray(drawn.astype(out[name].dtype))
    for name, factor in factors.items():
        out[name] = (out[name] * factor).astype(out[name].dtype)
    return out
```

```python
from collections import namedtuple
from contextlib import ExitStack

import numpy as np

import concourse.bass as bass
from concourse import mybir

F32 = mybir.dt.float32
F32R = mybir.dt.float32r
ALU = mybir.AluOpType
ACT = mybir.ActivationFunctionType
AX = mybir.AxisListType.X

P = 128
S = 512
D = 1024
DK = D // P
TB = S // P
F_FF = 2816
FC = F_FF // P
PARTS = (8, 8, 6)
HEADS = 4
AH, AD = 8, 64
TAPS_GDN, TAPS_FF, TAPS_DW = 4, 3, 31
WINDOWS = (2, 4, 8, 16)
EPS = 1e-6
PE_TAPS = 12
SCORE_BANKS = (0, 1, 5)
BLK = DK * P
RING = 4
AHEAD = 3
NEG = -3.0e38
LEVELS = 7

COLS = dict(attn_norm=DK, mlp_norm=DK, final_norm=DK, even_norm=DK, odd_norm=DK, ffn_norm0=DK, ffn_norm1=DK,
            ln_g=DK, ln_b=DK, dw_b=DK, pool_scale=len(WINDOWS), gdn_norm=1, q_norm=1, k_norm=1,
            a_log=1, dt_bias=1, b_f=1, gdn_conv=12 * TAPS_GDN, mlp_conv=2 * FC * TAPS_FF,
            ffn_conv0=2 * FC * TAPS_FF, ffn_conv1=2 * FC * TAPS_FF, ffn_bias0=2 * FC, ffn_bias1=2 * FC,
            dw=DK * TAPS_DW)
COL_AT, _at = {}, 0
for _n, _w in COLS.items():
    COL_AT[_n] = _at
    _at += _w
NCOLS = _at

CONSTS = dict(ones=P, ident=P, half_ones=P, causal=P, select=AH * P, count=len(WINDOWS) * 16)
CONST_AT, _at = {}, 0
for _n, _w in CONSTS.items():
    CONST_AT[_n] = _at
    _at += _w
NCONSTS = _at
MIX_CONSTS = dict(rotate=P, lower=P, upper=P, levels=LEVELS * P)
RET_CONSTS = dict(cos=S, sin=S, decay=HEADS * S)

STREAM = [("w_in", 32), ("w_out", 8)] + [("ff_a", 0)] + [("even_in", 16), ("even_out", 8)] + \
         [("ff_b", 0)] + [("pw1", 16), ("pw2", 8)] + [("ff_c", 0)]
NBLOCKS = sum(n for _, n in STREAM) + 3 * (2 * FC + DK * len(PARTS))


class Counts:

    def __init__(self, eng):
        self.eng, self.n, self.loop, self.last, self.waited = eng, {}, None, None, True

    def skip(self, sem, k=1, lag=0):
        self.n[(sem, lag)] = self.n.get((sem, lag), -lag) + k

    def now(self, sem, lag=0):
        key = (sem, lag)
        if self.loop and self.loop[1].get(key):
            return (self.loop[0] - 1) * self.loop[1][key] + self.n[key]
        return self.n[key]

    def next(self, sem, k=1):
        self.skip(sem, k)
        return self.now(sem)

    def passed(self, sem, lag, k=1):
        self.skip(sem, k, lag)
        return self.n[(sem, lag)] > 0

    def total(self, sem, lag=0):
        return self.n.get((sem, lag), -lag) + lag > 0

    def everything(self, sem, lag=0):
        return self.now(sem, lag) + lag

    def gave(self, sem):
        self.skip(sem)
        self.last, self.waited = sem, False
        return sem

    def unsettled(self):
        was, self.waited = self.waited, True
        return not was

    def repeat(self, times, body, once=()):
        before = dict(self.n)
        body(0)
        if self.unsettled():
            self.eng.wait_ge(self.last, self.now(self.last))
        grown = {k: v - before.get(k, -k[1]) for k, v in self.n.items()
                 if v != before.get(k, -k[1]) and k[0] not in once}
        if times > 1:
            with self.eng.Fori(1, times) as i:
                self.loop = (i, grown)
                start = dict(self.n)
                body(i)
                if self.unsettled():
                    self.eng.wait_ge(self.last, self.now(self.last))
                for k, g in grown.items():
                    assert self.n[k] - start[k] == g, (k, g)
                self.loop = None
            for k, g in grown.items():
                self.n[k] = start[k] + g * (times - 1)


SEMS = """x_ready cols_ready consts_ready small_ready mix_ready out_stored
 hi_ready lo_ready block_done evacuated added conv_done silu_done glu_done root_used act_hi act_ready
 sumsq_ready stat_done root_done norm_tmp norm_hi norm_ready small_split eps_ready vec_step act_step pool_step pe_step
 head_ready row_ready
 diag_ready pad_hi pad_ready taps_done taps_used tile_for_vec tile_for_act vec_for_pe act_for_pe vec_for_act act_for_vec
 pool_for_pe pool_for_act vec_for_pool pe_for_pool pool_for_vec act_for_pool""".split()


def names(**members):
    return namedtuple("Names", members)(**members)


def allocate(nc, ctx):
    def sb(name, shape, dt=F32):
        return ctx.enter_context(nc.sbuf_tensor(name, shape, dt))

    bank = [ctx.enter_context(nc.psum_tensor(f"bank{i}", [P, S], F32)) for i in range(8)]
    return names(
        res=sb("res", [P, DK, S]),
        nh=sb("nh", [P, DK, S], F32R), nl=sb("nl", [P, DK, S], F32R),
        raw=sb("raw", [P, RING, BLK]),
        wh=sb("wh", [P, RING, BLK], F32R), wl=sb("wl", [P, RING, BLK], F32R),
        cols=sb("cols", [P, NCOLS]), consts=sb("consts", [P, NCONSTS]),
        acc=sb("acc", [P, S]), rs=sb("rs", [P, S]), root=sb("root", [P, S]),
        sq=sb("sq", [P, 2, S]), tmp=sb("tmp", [P, 3, S]), eps=sb("eps", [P, 1]),
        bank=bank, stat=bank[4],
        raw_ready=[ctx.enter_context(nc.semaphore(f"raw_ready{i}")) for i in range(RING)],
        **{s: ctx.enter_context(nc.semaphore(s)) for s in SEMS})


def col(c, name, k=0, parts=P):
    at = COL_AT[name] + k
    return c.cols[0:parts, at:at + 1] if type(at) is int else c.cols[0:parts, bass.ds(at, 1)]


def const(c, name, parts=P):
    at = CONST_AT[name]
    return c.consts[0:parts, at:at + CONSTS[name]]


def piece(t, k, n=1):
    if type(k) is int:
        return t[:, k, :]
    return t[:, bass.ds(k, 1), :].rearrange("p a s -> p (a s)")


def heads_view(t, c0=None):
    return t.rearrange("p (h n) -> p h n", h=HEADS)


def over_heads(t):
    return t.unsqueeze(1).to_broadcast([P, HEADS, P])


def over_columns(t):
    return t.unsqueeze(2).to_broadcast([P, HEADS, P])



def tensor_program(c, m1, gd, ff, m2, cf, e):
    n = Counts(e)
    bank = c.bank

    def mm(out, lhsT, rhs, start, stop):
        return e.matmul(out, lhsT, rhs, start=start, stop=stop, skip_group_check=True)

    def split_product(out, wh, wl, xh, xl, start, stop):
        mm(out, wh, xh, start, False)
        mm(out, wh, xl, False, False)
        return mm(out, wl, xh, False, stop)

    def block(j, xh, xl, nk):
        e.wait_ge(c.lo_ready, n.next(c.lo_ready))
        for k in range(nk):
            last = split_product(bank[j][:, :], c.wh[:, j, k * P:(k + 1) * P], c.wl[:, j, k * P:(k + 1) * P],
                                 xh[:, k, :], xl[:, k, :], k == 0, k == nk - 1)
        last.then_inc(n.gave(c.block_done), 1)

    def first_pair(xh, xl, nk, ready):
        e.wait_ge(c.lo_ready, n.next(c.lo_ready, k=2))
        for k in range(nk):
            e.wait_ge(ready, n.next(ready))
            for j in range(2):
                last = split_product(bank[j][:, :], c.wh[:, j, k * P:(k + 1) * P], c.wl[:, j, k * P:(k + 1) * P],
                                     xh[:, k, :], xl[:, k, :], k == 0, k == nk - 1)
                if k == nk - 1:
                    last.then_inc(n.gave(c.block_done), 1)

    def project(blocks, first=False):
        if n.total(c.added, lag=RING):
            e.wait_ge(c.added, n.everything(c.added, lag=RING))

        def body(i):
            for j in range(RING):
                if n.passed(c.evacuated, lag=RING):
                    e.wait_ge(c.evacuated, n.now(c.evacuated, lag=RING))
                if not (first and type(i) is int and i == 0 and j < 2):
                    block(j, c.nh, c.nl, DK)
                elif j == 1:
                    first_pair(c.nh, c.nl, DK, c.norm_ready)
        n.repeat(blocks // RING, body, once=(c.norm_ready,))

    def reduce_into_residual(xh, xl, nk, ready):
        if n.total(c.evacuated, lag=RING):
            e.wait_ge(c.evacuated, n.everything(c.evacuated, lag=RING))

        def body(i):
            for j in range(RING):
                if n.passed(c.added, lag=RING):
                    e.wait_ge(c.added, n.now(c.added, lag=RING))
                if not (type(i) is int and i == 0 and j < 2):
                    block(j, xh, xl, nk)
                elif j == 1:
                    first_pair(xh, xl, nk, ready)
        n.repeat(DK // RING, body, once=(ready,))

    def project_tokens():
        for w in range(RING):
            e.wait_ge(c.lo_ready, n.next(c.lo_ready))
            for t in range(TB):
                if w == 0:
                    if n.passed(c.evacuated, lag=RING):
                        e.wait_ge(c.evacuated, n.now(c.evacuated, lag=RING))
                for k in (2 * w, 2 * w + 1):
                    ts, ws = slice(t * P, (t + 1) * P), slice((k % 2) * S, (k % 2 + 1) * S)
                    last = split_product(bank[t][:, :], c.nh[:, k, ts], c.nl[:, k, ts],
                                         c.wh[:, w, ws], c.wl[:, w, ws], k == 0, k == DK - 1)
            last.then_inc(n.gave(c.block_done), 1)

    def rows(w):
        e.wait_ge(c.small_split, n.next(c.small_split))
        for k in range(DK):
            last = split_product(bank[4][:, :], w[0][:, k, :], w[1][:, k, :], c.nh[:, k, :], c.nl[:, k, :],
                                 k == 0, k == DK - 1)
        last.then_inc(n.gave(c.tile_for_vec), 1)

    def column_sum():
        e.wait_ge(c.sumsq_ready, n.next(c.sumsq_ready))
        mm(c.stat[:, :], const(c, "ones"), c.acc[:, :], True, True).then_inc(n.gave(c.stat_done), 1)

    def slice_stats(count, ones):
        for h in range(count):
            e.wait_ge(c.act_for_pe, n.next(c.act_for_pe))
            mm(bank[4 + h % 4][:, :], ones, c.sq[:, h % 2, :], True, True).then_inc(n.gave(c.tile_for_act), 1)

    def feed_forward():
        for at, part in enumerate(PARTS):
            project(2 * part, first=at == 0)
            reduce_into_residual(ff.ah, ff.al, part, c.act_ready)

    def retention():
        project_rope()
        project_tokens()
        project(4)
        if n.total(c.vec_for_pe):
            e.wait_ge(c.vec_for_pe, n.everything(c.vec_for_pe))
        if n.total(c.evacuated, lag=RING):
            e.wait_ge(c.evacuated, n.everything(c.evacuated, lag=RING))
        steps = [(h, j) for h in range(HEADS) for j in range(TB)]
        for at in range(len(steps) + 2):
            if at < len(steps):
                h, j = steps[at]
                mm(bank[5 + at % 3][:, 0:S - j * P], m1.rk[:, h, j * P:(j + 1) * P],
                          m1.rq[:, h, j * P:S], True, True).then_inc(n.gave(c.tile_for_vec), 1)
            if at >= 2:
                h, j = steps[at - 2]
                e.wait_ge(c.vec_for_pe, n.next(c.vec_for_pe))
                last = mm(bank[h][:, j * P:S], m1.rv[:, j, h * P:(h + 1) * P],
                          m1.pt[:, (at - 2) % 3, 0:S - j * P], j == 0, j == TB - 1)
                if j == TB - 1:
                    last.then_inc(n.gave(c.tile_for_act), 1)
        slice_stats(HEADS, const(c, "ones"))

    def project_rope():
        e.wait_ge(c.mix_ready, n.next(c.mix_ready, k=32))
        """Queries and keys; the channel-pair swap of slice s follows the products of slice s + 1."""
        def swap(s):
            e.wait_ge(c.evacuated, n.next(c.evacuated))
            t = m1.rq if s < HEADS else m1.rk
            if n.passed(c.vec_for_pe, lag=2):
                e.wait_ge(c.vec_for_pe, n.now(c.vec_for_pe, lag=2))
            mm(bank[5 + s % 2][:, :], m1.rotate[:, :], t[:, s % HEADS, :], True, True).then_inc(n.gave(c.tile_for_vec), 1)
        for s in range(2 * HEADS):
            if n.passed(c.evacuated, lag=RING):
                e.wait_ge(c.evacuated, n.now(c.evacuated, lag=RING))
            if s >= 2:
                block(s % RING, c.nh, c.nl, DK)
            elif s == 1:
                first_pair(c.nh, c.nl, DK, c.norm_ready)
            if s >= 1:
                swap(s - 1)
        swap(2 * HEADS - 1)
        n.n[(c.vec_for_pe, 0)] = 2 * HEADS

    def delta_net():
        project(12)
        rows((gd.wh, gd.wl))
        slice_stats(2 * HEADS, const(c, "ones"))
        e.wait_ge(c.vec_for_pe, n.next(c.vec_for_pe, k=2))
        for t in range(TB):
            last = e.transpose(bank[5][:, t * 64:(t + 1) * 64], gd.rows[0:64, t * P:(t + 1) * P],
                               const(c, "ident", 64)[:, 0:64])
        last.then_inc(n.gave(c.tile_for_act), 1)
        if n.total(c.evacuated, lag=RING):
            e.wait_ge(c.evacuated, n.everything(c.evacuated, lag=RING))
        for h in range(HEADS):
            last = mm(bank[h][:, :], const(c, "select", 64)[:, h * P:(h + 1) * P], gd.rows[0:64, :], True, True)
            last.then_inc(n.gave(c.tile_for_act), 1)
        e.wait_ge(c.act_for_pe, n.next(c.act_for_pe, k=HEADS))
        for t in range(TB):
            cs = slice(t * P, (t + 1) * P)

            def heads(b, fn):
                for h in range(HEADS):
                    last = fn(h, bank[b][:, h * P:(h + 1) * P])
                return last

            heads(0, lambda h, o: e.transpose(o, gd.k[:, h, cs], const(c, "ident"))).then_inc(n.gave(c.tile_for_vec), 1)
            heads(1, lambda h, o: e.transpose(o, gd.v[:, h, cs], const(c, "ident"))).then_inc(n.gave(c.tile_for_vec), 1)
            heads(2, lambda h, o: mm(o, gd.k[:, h, cs], gd.k[:, h, cs], True, True)).then_inc(n.gave(c.tile_for_vec), 1)
            heads(3, lambda h, o: mm(o, gd.k[:, h, cs], gd.q[:, h, cs], True, True)).then_inc(n.gave(c.tile_for_vec), 1)
            hs = [slice(h * P, (h + 1) * P) for h in range(HEADS)]
            e.wait_ge(c.vec_for_pe, n.next(c.vec_for_pe))
            heads(4, lambda h, o: e.transpose(o, gd.lev[:, 0, hs[h]], const(c, "ident"))).then_inc(n.gave(c.tile_for_vec), 1)
            for lv in range(1, LEVELS):
                e.wait_ge(c.vec_for_pe, n.next(c.vec_for_pe))
                heads(4, lambda h, o: mm(o, gd.lev[:, lv % 2, hs[h]], gd.U[:, hs[h]], True, True)).then_inc(n.gave(c.tile_for_act), 1)
                e.wait_ge(c.act_for_pe, n.next(c.act_for_pe))
                if lv < LEVELS - 1:
                    heads(5, lambda h, o: mm(o, gd.Z[:, hs[h]], gd.T[:, hs[h]], True, True)).then_inc(n.gave(c.tile_for_vec), 1)
                heads(6, lambda h, o: mm(o, gd.T[:, hs[h]], gd.Z[:, hs[h]], True, True)).then_inc(n.gave(c.tile_for_vec), 1)
            e.wait_ge(c.vec_for_pe, n.next(c.vec_for_pe))
            if t > 0:
                heads(7, lambda h, o: mm(o, gd.kbg[:, hs[h]], gd.U[:, hs[h]], True, True)).then_inc(n.gave(c.tile_for_act), 1)
                e.wait_ge(c.act_for_pe, n.next(c.act_for_pe))
            for h in range(HEADS):
                o = bank[0][:, hs[h]]
                last = mm(o, gd.U[:, hs[h]], gd.vb[:, hs[h]], True, t == 0)
                if t > 0:
                    last = mm(o, gd.nw[:, hs[h]], gd.state[:, hs[h]], False, True)
            last.then_inc(n.gave(c.tile_for_act), 1)
            e.wait_ge(c.act_for_pe, n.next(c.act_for_pe))
            for h in range(HEADS):
                o = bank[1][:, hs[h]]
                if t > 0:
                    mm(o, gd.state[:, hs[h]], gd.qd[:, hs[h]], True, False)
                last = mm(o, gd.u[:, hs[h]], gd.qk[:, hs[h]], t == 0, True)
            last.then_inc(n.gave(c.tile_for_act), 1)
            if t < TB - 1:
                heads(2, lambda h, o: mm(o, gd.kd[:, hs[h]], gd.u[:, hs[h]], True, True)).then_inc(n.gave(c.tile_for_vec), 1)
                e.wait_ge(c.vec_for_pe, n.next(c.vec_for_pe))
            e.wait_ge(c.act_for_pe, n.next(c.act_for_pe))
        project(4)
        slice_stats(HEADS, const(c, "ones"))

    def depthwise():
        e.wait_ge(c.added, n.everything(c.added, lag=RING))

        def body(i):
            for j in range(RING):
                if n.passed(c.evacuated, lag=RING):
                    e.wait_ge(c.evacuated, n.now(c.evacuated, lag=RING))
                if not (type(i) is int and i == 0 and j < 2):
                    block(j, c.nh, c.nl, DK)
                elif j == 1:
                    first_pair(c.nh, c.nl, DK, c.norm_ready)
            for q in range(2):
                e.wait_ge(c.diag_ready, n.next(c.diag_ready))
                e.wait_ge(c.pad_ready, n.next(c.pad_ready))
                if n.passed(c.taps_used, lag=2):
                    e.wait_ge(c.taps_used, n.now(c.taps_used, lag=2))
                for tap in range(PE_TAPS):
                    last = split_product(bank[5 + q][:, :], cf.diag_h[:, q, tap, :], cf.diag_l[:, q, tap, :],
                                         cf.pad_h[:, q, tap:tap + S], cf.pad_l[:, q, tap:tap + S],
                                         tap == 0, tap == PE_TAPS - 1)
                last.then_inc(n.gave(c.taps_done), 1)
        n.repeat(DK // 2, body, once=(c.norm_ready,))

    def attention():
        project(8, first=True)
        project_tokens()
        project(4)
        rows((m2.wh, m2.wl))
        slice_stats(8, const(c, "half_ones"))
        e.wait_ge(c.vec_for_pe, n.next(c.vec_for_pe, k=2))
        for t in range(TB):
            last = e.transpose(bank[5][:, t * AH:(t + 1) * AH], m2.rows[0:AH, t * P:(t + 1) * P],
                               const(c, "ident", AH)[:, 0:AH])
        last.then_inc(n.gave(c.tile_for_act), 1)
        e.wait_ge(c.act_for_pe, n.next(c.act_for_pe))
        steps = [(h, t) for h in range(AH) for t in range(TB)]

        def scores(at):
            h, t = steps[at]
            lo = (h % 2) * AD
            if t == 0:
                if n.passed(c.row_ready, lag=1):
                    e.wait_ge(c.row_ready, n.now(c.row_ready, lag=1))
                mm(bank[4][:, :], const(c, "select", AH)[:, h * P:(h + 1) * P], m2.rows[0:AH, :],
                          True, True).then_inc(n.gave(c.tile_for_act), 1)
            w = (t + 1) * P
            mm(bank[SCORE_BANKS[at % 3]][:, 0:w], m2.q[lo:lo + AD, h // 2, t * P:w], m2.k[lo:lo + AD, h // 2, 0:w],
                      True, True).then_inc(n.gave(c.tile_for_vec), 1)

        def weigh(at):
            h, t = steps[at]
            e.wait_ge(c.vec_for_pe, n.next(c.vec_for_pe))
            for j in range(t + 1):
                last = e.transpose(bank[2 + at % 2][:, j * P:(j + 1) * P], m2.p[:, at % 3, j * P:(j + 1) * P],
                                   const(c, "ident"))
            last.then_inc(n.gave(c.tile_for_act), 1)

        def output(at):
            h, t = steps[at]
            e.wait_ge(c.act_for_pe, n.next(c.act_for_pe))
            for j in range(t + 1):
                last = mm(bank[6 + h % 2][:, t * P:(t + 1) * P],
                          m2.v[:, j, (h // 2) * P:(h // 2 + 1) * P], m2.pt[:, at % 2, j * P:(j + 1) * P],
                          j == 0, j == t)
            if t == TB - 1:
                last.then_inc(n.gave(c.tile_for_act), 1)

        scores(0)
        scores(1)
        for at in range(len(steps)):
            if at + 2 < len(steps):
                scores(at + 2)
            weigh(at)
            if at >= 1:
                output(at - 1)
        output(len(steps) - 1)
        for g in range(len(WINDOWS)):
            e.wait_ge(c.vec_for_pe, n.next(c.vec_for_pe))
            mm(bank[g][:, :], m2.wpool[:, g, :], m2.q[:, g, :], True, True).then_inc(n.gave(c.tile_for_act), 1)
        e.wait_ge(c.act_for_pe, n.next(c.act_for_pe))

    e.wait_ge(c.consts_ready, n.next(c.consts_ready, k=16))
    column_sum()
    retention()
    delta_net()
    reduce_into_residual(c.nh, c.nl, DK, c.norm_ready)
    column_sum()
    feed_forward()
    column_sum()
    column_sum()
    attention()
    reduce_into_residual(c.nh, c.nl, DK, c.norm_ready)
    column_sum()
    feed_forward()
    column_sum()
    depthwise()
    column_sum()
    column_sum()
    reduce_into_residual(c.nh, c.nl, DK, c.norm_ready)
    column_sum()
    feed_forward()



def scalar_program(c, m1, gd, ff, m2, cf, e):
    n = Counts(e)
    bank = c.bank
    state = dict(split=0)

    def act(out, in_, func, **kw):
        if n.unsettled():
            e.wait_ge(n.last, n.now(n.last))
        return e.activation(out, in_, func, **kw)

    def split():
        if state["split"] == NBLOCKS:
            return
        j = state["split"] % RING
        state["split"] += 1
        e.wait_ge(c.raw_ready[j], n.next(c.raw_ready[j], k=16))
        if n.passed(c.block_done, lag=RING):
            e.wait_ge(c.block_done, n.now(c.block_done, lag=RING))
        act(c.wh[:, j, :], c.raw[:, j, :], ACT.Copy).then_inc(n.gave(c.hi_ready), 1)

    def groups(blocks, body):
        def counted(i):
            was = state["split"]
            body(i)
            state["split"] = was + RING
        times = blocks // RING
        last = state["split"] + blocks > NBLOCKS
        if times - last > 0:
            start = state["split"]
            n.repeat(times - last, counted)
            state["split"] = start + (times - last) * RING
        if last:
            body(times - 1)

    def arrived():
        e.wait_ge(c.block_done, n.next(c.block_done))

    def evacuate(blocks, place, func=ACT.Copy, after=None):
        def body(i):
            for j in range(RING):
                split()
                arrived()
                act(place(RING * i + j, j), bank[j][:, :], func).then_inc(n.gave(c.evacuated), 1)
                if after:
                    after(RING * i + j, j)
        groups(blocks, body)

    def residual():
        def body(i):
            for j in range(RING):
                split()
                n.skip(c.block_done)
        groups(DK, body)

    def tokens(dest):
        for j in range(RING):
            split()
            arrived()
        for t in range(TB):
            act(dest[:, t, :], bank[t][:, :], ACT.Copy).then_inc(n.gave(c.evacuated), 1)

    def inverse_root(scale):
        e.wait_ge(c.stat_done, n.next(c.stat_done))
        act(c.root[:, :], c.stat[:, :], ACT.Ln, bias=c.eps[:, 0:1], scale=scale).then_inc(n.gave(c.act_step), 1)
        act(c.root[:, :], c.root[:, :], ACT.Exp, scale=-0.5).then_inc(n.gave(c.root_done), 1)

    def norm_split():
        inverse_root(1.0 / D)
        for k in range(DK):
            e.wait_ge(c.norm_tmp, n.next(c.norm_tmp))
            act(c.nh[:, k, :], c.tmp[:, k % 3, :], ACT.Copy).then_inc(n.gave(c.norm_hi), 1)

    def squares(src):
        for k in range(DK):
            e.wait_ge(c.vec_for_act, n.next(c.vec_for_act))
            act(c.sq[:, k % 2, :], src(k), ACT.Square).then_inc(n.gave(c.act_for_vec), 1)

    def split_mix(mix):
        e.wait_ge(c.vec_for_act, n.next(c.vec_for_act))
        for k in range(DK):
            act(c.nh[:, k, :], mix[:, k, :], ACT.Copy).then_inc(n.gave(c.norm_hi), 1)

    def slice_roots(count, src, scale):
        for first in range(0, count, 4):
            for h in range(first, first + 5):
                if h < first + 4:
                    act(c.sq[:, h % 2, :], src(h), ACT.Square).then_inc(n.gave(c.act_for_pe), 1)
                if h > first:
                    e.wait_ge(c.tile_for_act, n.next(c.tile_for_act))
                    total = bank[4 + (h - 1) % 4][:, :]
                    act(total, total, ACT.Ln, bias=c.eps[:, 0:1], scale=scale).then_inc(n.gave(c.act_step), 1)
            for h in range(first, first + 4):
                if n.passed(c.root_used, lag=2):
                    e.wait_ge(c.root_used, n.now(c.root_used, lag=2))
                act(c.tmp[:, h % 2, :], bank[4 + h % 4][:, :], ACT.Exp,
                    scale=-0.5).then_inc(n.gave(c.act_for_vec), 1)

    def feed_forward():
        def pairs(i, part):
            for q in range(2):
                f = 2 * i + q
                for j in (2 * q, 2 * q + 1):
                    split()
                    arrived()
                    if n.passed(c.conv_done, lag=4):
                        e.wait_ge(c.conv_done, n.now(c.conv_done, lag=4))
                    act(ff.pad[:, j, TAPS_FF - 1:], bank[j][:, :], ACT.Copy).then_inc(n.gave(c.evacuated), 1)
                e.wait_ge(c.conv_done, n.next(c.conv_done))
                act(ff.gate[:, q, :], ff.conv[:, 2 * q, :], ACT.Silu).then_inc(n.gave(c.silu_done), 1)
                n.skip(c.conv_done)
                e.wait_ge(c.glu_done, n.next(c.glu_done))
                act(piece(ff.ah, f), ff.glu[:, q, :], ACT.Copy).then_inc(n.gave(c.act_hi), 1)
        for part in PARTS:
            groups(2 * part, lambda i: pairs(i, part))
            residual()

    def log_sigmoid_terms(t, src, parts):
        e.wait_ge(c.vec_for_act, n.next(c.vec_for_act))
        act(t[0:parts, 2, :], src, ACT.Exp, scale=-1.0).then_inc(n.gave(c.act_step), 1)
        act(t[0:parts, 2, :], t[0:parts, 2, :], ACT.Ln, bias=1.0).then_inc(n.gave(c.act_step), 1)

    e.wait_ge(c.eps_ready, n.next(c.eps_ready))
    e.wait_ge(c.cols_ready, n.next(c.cols_ready, k=16))
    for _ in range(AHEAD):
        split()
    norm_split()
    for b in range(8):
        split()
        arrived()
        act((m1.rq if b < HEADS else m1.rk)[:, b % HEADS, :], bank[b % RING][:, :], ACT.Copy).then_inc(n.gave(c.evacuated), 1)
    tokens(m1.rv)
    evacuate(4, lambda b, j: m1.rg[:, j, :], ACT.Silu)
    for h in range(HEADS):
        e.wait_ge(c.tile_for_act, n.next(c.tile_for_act))
        act(m1.mix[:, HEADS + h, :], bank[h][:, :], ACT.Copy).then_inc(n.gave(c.act_step), 1)
    slice_roots(HEADS, lambda h: m1.mix[:, HEADS + h, :], 1.0 / P)
    def gdn_slice(b, j):
        t = (gd.q, gd.k, gd.v)[b // HEADS][:, b % HEADS, :]
        e.wait_ge(c.conv_done, n.next(c.conv_done))
        act(t, t, ACT.Silu).then_inc(n.gave(c.act_step), 1)
    e.wait_ge(c.vec_for_act, n.next(c.vec_for_act))
    for b in range(12):
        split()
        arrived()
        if n.passed(c.conv_done, lag=4):
            e.wait_ge(c.conv_done, n.now(c.conv_done, lag=4))
        act(gd.pad[:, b % RING, TAPS_GDN - 1:], bank[b % RING][:, :], ACT.Copy).then_inc(n.gave(c.evacuated), 1)
        gdn_slice(b, b % RING)
    e.wait_ge(c.small_ready, n.next(c.small_ready, k=16))
    act(gd.wh[:, :, :], gd.w[:, :, :], ACT.Copy).then_inc(n.gave(c.act_for_vec), 1)
    e.wait_ge(c.vec_for_act, n.next(c.vec_for_act))
    act(gd.rows[32:32 + HEADS, :], gd.ab[32:32 + HEADS, :], ACT.Sigmoid).then_inc(n.gave(c.act_step), 1)
    act(gd.ea[0:HEADS, :], col(c, "a_log", parts=HEADS), ACT.Exp).then_inc(n.gave(c.act_step), 1)
    log_sigmoid_terms(c.tmp, c.tmp[0:HEADS, 1, :], HEADS)
    act(gd.ea[0:HEADS, :], gd.ea[0:HEADS, :], ACT.Copy).then_inc(n.gave(c.act_for_vec), 1)
    e.wait_ge(c.vec_for_act, n.next(c.vec_for_act))
    slice_roots(8, lambda h: (gd.q if h < HEADS else gd.k)[:, h % HEADS, :], 1.0)
    e.wait_ge(c.tile_for_act, n.next(c.tile_for_act))
    act(gd.cols[:, :, :].rearrange("p t r -> p (t r)"), bank[5][:, 0:TB * 64], ACT.Copy).then_inc(n.gave(c.act_step), 1)
    for h in range(HEADS):
        e.wait_ge(c.tile_for_act, n.next(c.tile_for_act))
        act(gd.gr[:, h, :], bank[h][:, :], ACT.Copy).then_inc(n.gave(c.act_for_pe), 1)
    last = gd.gr.rearrange("p h (t s) -> p t h s", s=P)[:, :, :, P - 1]
    act(gd.egc[:, :, :], gd.cols[:, :, 0:HEADS], ACT.Exp).then_inc(n.gave(c.act_step), 1)
    act(gd.cd[:, :, :], last, ACT.Exp).then_inc(n.gave(c.act_for_vec), 1)
    e.wait_ge(c.vec_for_act, n.next(c.vec_for_act))
    act(gd.kds[:, :, :], gd.dl[:, :, :], ACT.Exp).then_inc(n.gave(c.act_for_vec), 1)
    for t in range(TB):
        cs = slice(t * P, (t + 1) * P)
        e.wait_ge(c.vec_for_act, n.next(c.vec_for_act))
        act(gd.dec[:, 0, :], c.tmp[:, 1, :], ACT.Exp, scale=-1.0).then_inc(n.gave(c.act_for_vec), 1)
        act(gd.dec[:, 1, :], c.tmp[:, 2, :], ACT.Exp).then_inc(n.gave(c.act_for_vec), 1)
        act(heads_view(gd.eg[:, :]), gd.gr[:, :, cs], ACT.Exp).then_inc(n.gave(c.act_for_vec), 1)
        for lv in range(1, LEVELS):
            e.wait_ge(c.tile_for_act, n.next(c.tile_for_act))
            act(gd.Z[:, :], bank[4][:, :], ACT.Copy).then_inc(n.gave(c.act_for_pe), 1)
        if t > 0:
            e.wait_ge(c.tile_for_act, n.next(c.tile_for_act))
            act(gd.nw[:, :], bank[7][:, :], ACT.Copy, scale=-1.0).then_inc(n.gave(c.act_for_pe), 1)
        e.wait_ge(c.tile_for_act, n.next(c.tile_for_act))
        act(gd.u[:, :], bank[0][:, :], ACT.Copy).then_inc(n.gave(c.act_for_pe), 1)
        e.wait_ge(c.tile_for_act, n.next(c.tile_for_act))
        act(m1.mix[:, 0:HEADS, cs], heads_view(bank[1][:, :]), ACT.Copy).then_inc(n.gave(c.act_for_pe), 1)
    evacuate(4, lambda b, j: gd.gr[:, j, :], ACT.Silu)
    slice_roots(HEADS, lambda h: m1.mix[:, h, :], 1.0 / P)
    split_mix(m1.mix)
    residual()
    norm_split()
    feed_forward()
    inverse_root(1.0 / D)
    squares(lambda k: c.res[:, k, :])
    norm_split()
    for b in range(8):
        split()
        arrived()
        act((m2.q if b < HEADS else m2.k)[:, b % HEADS, :], bank[b % RING][:, :], ACT.Copy).then_inc(n.gave(c.evacuated), 1)
    tokens(m2.v)
    evacuate(4, lambda b, j: m2.pool[:, j, 16:])
    e.wait_ge(c.small_ready, n.next(c.small_ready, k=32))
    act(m2.wh[:, :, :], m2.w[:, :, :], ACT.Copy).then_inc(n.gave(c.act_for_vec), 1)
    log_sigmoid_terms(c.tmp, c.tmp[0:AH, 1, :], AH)
    act(c.tmp[0:AH, 2, :], c.tmp[0:AH, 2, :], ACT.Copy).then_inc(n.gave(c.act_for_vec), 1)
    e.wait_ge(c.vec_for_act, n.next(c.vec_for_act))
    slice_roots(8, lambda h: (m2.q if h < HEADS else m2.k)[:, h % HEADS, :], 1.0 / AD)
    e.wait_ge(c.tile_for_act, n.next(c.tile_for_act))
    act(m2.ccol[:, :], bank[5][:, 0:TB * AH], ACT.Copy).then_inc(n.gave(c.act_for_pe), 1)
    steps = [(h, t) for h in range(AH) for t in range(TB)]

    def forget_row(at):
        h, t = steps[at]
        if t == 0:
            e.wait_ge(c.tile_for_act, n.next(c.tile_for_act))
            act(m2.nrow[:, h % 2, :], bank[4][:, :], ACT.Copy, scale=-1.0).then_inc(n.gave(c.row_ready), 1)

    def softmax(at):
        h, t = steps[at]
        e.wait_ge(c.vec_for_act, n.next(c.vec_for_act))
        act(m2.p[:, at % 3, 0:(t + 1) * P], m2.s[:, at % 3, 0:(t + 1) * P], ACT.Exp,
            bias=m2.nmax[:, at % 3:at % 3 + 1], accum_out=m2.sum[:, at % 3:at % 3 + 1]).then_inc(n.gave(c.act_for_vec), 1)

    def head_output(h):
        lo = (h % 2) * AD
        e.wait_ge(c.tile_for_act, n.next(c.tile_for_act))
        act(m2.mix[lo:lo + AD, h // 2, :], bank[6 + h % 2][lo:lo + AD, :], ACT.Copy).then_inc(n.gave(c.act_step), 1)

    forget_row(0)
    softmax(0)
    softmax(1)
    for at, (h, t) in enumerate(steps):
        if at + 2 < len(steps):
            forget_row(at + 2)
        e.wait_ge(c.tile_for_act, n.next(c.tile_for_act))
        act(m2.pt[:, at % 2, 0:(t + 1) * P], bank[2 + at % 2][:, 0:(t + 1) * P], ACT.Copy).then_inc(n.gave(c.act_for_pe), 1)
        if at and t == 0:
            head_output(h - 1)
        if at + 2 < len(steps):
            softmax(at + 2)
    head_output(AH - 1)
    for g in range(len(WINDOWS)):
        e.wait_ge(c.tile_for_act, n.next(c.tile_for_act))
        act(m2.mix[:, HEADS + g, :], bank[g][:, :], ACT.Identity,
            scale=col(c, "pool_scale", g)).then_inc(n.gave(c.act_for_pe if g == 3 else c.act_step), 1)
    for k in range(DK):
        act(c.nh[:, k, :], m2.mix[:, k, :], ACT.Copy).then_inc(n.gave(c.norm_hi), 1)
    residual()
    norm_split()
    feed_forward()
    norm_split()
    dw_at = COL_AT["dw"]
    act(cf.dw_h[:, :], c.cols[:, dw_at:dw_at + DK * TAPS_DW], ACT.Copy).then_inc(n.gave(c.act_for_vec), 1)
    e.wait_ge(c.vec_for_act, n.next(c.vec_for_act))

    def glu(i):
        pair = bass.ds(2 * i * TAPS_DW, 2 * TAPS_DW)
        act(cf.tap_h[:, :], cf.dw_h[:, pair].bitcast(F32), ACT.Copy).then_inc(n.gave(c.act_step), 1)
        act(cf.tap_l[:, :], cf.dw_l[:, pair], ACT.Copy).then_inc(n.gave(c.act_step), 1)

        def high(q):
            e.wait_ge(c.glu_done, n.next(c.glu_done))
            act(cf.pad_h[:, q, :], cf.pad[:, q, :], ACT.Copy).then_inc(n.gave(c.pad_hi), 1)

        for q in range(2):
            split()
            arrived()
            if n.passed(c.glu_done, lag=2):
                e.wait_ge(c.glu_done, n.now(c.glu_done, lag=2))
            act(cf.val[:, q, :], bank[2 * q][:, :], ACT.Copy).then_inc(n.gave(c.evacuated), 1)
            split()
            arrived()
            act(cf.gate[:, q, :], bank[2 * q + 1][:, :], ACT.Sigmoid).then_inc(n.gave(c.evacuated), 1)
            if q == 1:
                high(0)
            if n.passed(c.taps_done, lag=2):
                e.wait_ge(c.taps_done, n.now(c.taps_done, lag=2))
            for tap in range(PE_TAPS):
                at = q * TAPS_DW + tap
                for diag, dw in ((cf.diag_h, cf.tap_h), (cf.diag_l, cf.tap_l)):
                    last = diag is cf.diag_l and tap == PE_TAPS - 1
                    e.activation(diag[:, q, tap, :], const(c, "ident"), ACT.Copy,
                                 scale=dw[:, at:at + 1]).then_inc(n.gave(c.diag_ready if last else c.act_step), 1)
        high(1)
    n.n[(c.glu_done, 2)] = n.n[(c.glu_done, 0)] - 2
    groups(16, glu)
    e.wait_ge(c.stat_done, n.next(c.stat_done))
    act(c.root[:, :], c.stat[:, :], ACT.Copy, scale=1.0 / D).then_inc(n.gave(c.root_done), 1)
    squares(lambda k: cf.u[:, k, :])
    inverse_root(1.0 / D)
    for k in range(DK):
        e.wait_ge(c.norm_tmp, n.next(c.norm_tmp))
        if k >= 2:
            if n.total(c.norm_hi):
                e.wait_ge(c.norm_hi, n.everything(c.norm_hi))
        act(cf.y[:, k % 2, :], c.tmp[:, k % 3, :], ACT.Silu, bias=col(c, "ln_b", k),
            scale=col(c, "ln_g", k)).then_inc(n.gave(c.act_step), 1)
        act(c.nh[:, k, :], cf.y[:, k % 2, :], ACT.Copy).then_inc(n.gave(c.norm_hi), 1)
    residual()
    norm_split()
    feed_forward()



def vector_program(c, m1, gd, ff, m2, cf, e):
    n = Counts(e)
    bank = c.bank

    def tt(out, a, b, op):
        if n.unsettled():
            e.wait_ge(n.last, n.now(n.last))
        return e.tensor_tensor(out, a, b, op)

    def ts(out, a, s1, s2, op0, op1):
        if n.unsettled():
            e.wait_ge(n.last, n.now(n.last))
        return e.tensor_scalar(out, a, s1, s2, op0) if op1 is None else e.tensor_scalar(out, a, s1, s2, op0, op1)

    def stt(out, a, s, b, op0, op1):
        if n.unsettled():
            e.wait_ge(n.last, n.now(n.last))
        return e.scalar_tensor_tensor(out=out, in0=a, scalar=s, in1=b, op0=op0, op1=op1)

    def clear(t):
        if n.unsettled():
            e.wait_ge(n.last, n.now(n.last))
        e.memset(t, 0.0).then_inc(n.gave(c.vec_step), 1)

    def tell(sem):
        if n.unsettled():
            e.wait_ge(n.last, n.now(n.last))
        e.sem_inc(sem, 1)
        n.skip(sem)

    def add_square(x, j):
        tt(c.sq[:, j % 2, :], x, x, ALU.mult).then_inc(n.gave(c.vec_step), 1)
        tt(c.acc[:, :], c.acc[:, :], c.sq[:, j % 2, :], ALU.add).then_inc(n.gave(c.vec_step), 1)

    def residual(stats=True):
        if stats:
            clear(c.acc[:, :])

        def body(i):
            for j in range(RING):
                e.wait_ge(c.block_done, n.next(c.block_done))
                x = piece(c.res, RING * i + j)
                tt(x, bank[j][:, :], x, ALU.add).then_inc(n.gave(c.added), 1)
                if stats:
                    add_square(x, j)
        n.repeat(DK // RING, body)
        if stats:
            tell(c.sumsq_ready)

    def norm_split(name):
        e.wait_ge(c.root_done, n.next(c.root_done))
        for k in range(DK + 1):
            if k < DK:
                stt(c.tmp[:, k % 3, :], c.res[:, k, :], col(c, name, k), c.root[:, :], ALU.mult, ALU.mult).then_inc(n.gave(c.norm_tmp), 1)
            if k >= 1:
                e.wait_ge(c.norm_hi, n.next(c.norm_hi))
                tt(c.nl[:, k - 1, :], c.tmp[:, (k - 1) % 3, :], c.nh[:, k - 1, :].bitcast(F32), ALU.subtract).then_inc(n.gave(c.norm_ready), 1)

    def low_parts(mix):
        for k in range(DK):
            e.wait_ge(c.norm_hi, n.next(c.norm_hi))
            tt(c.nl[:, k, :], mix[:, k, :], c.nh[:, k, :].bitcast(F32), ALU.subtract).then_inc(n.gave(c.norm_ready), 1)

    def convolve(y, x, taps, name, at, bias):
        last = taps - 1
        if bias is None:
            ts(y, x[:, last:last + S], col(c, name, at + last), None, ALU.mult, None).then_inc(n.gave(c.vec_step), 1)
        else:
            ts(y, x[:, last:last + S], col(c, name, at + last), bias, ALU.mult, ALU.add).then_inc(n.gave(c.vec_step), 1)
        for tap in range(last - 1, -1, -1):
            stt(y, x[:, tap:tap + S], col(c, name, at + tap), y, ALU.mult, ALU.add).then_inc(n.gave(c.conv_done if tap == 0 and taps != TAPS_DW else c.vec_step), 1)

    def slice_scale(x, scalar):
        e.wait_ge(c.act_for_vec, n.next(c.act_for_vec))
        h = slice_scale.count % 2
        slice_scale.count += 1
        if scalar is None:
            tt(x, x, c.tmp[:, h, :], ALU.mult).then_inc(n.gave(c.root_used), 1)
        else:
            stt(x, x, scalar, c.tmp[:, h, :], ALU.mult, ALU.mult).then_inc(n.gave(c.root_used), 1)
    slice_scale.count = 0

    def feed_forward(conv, bias, stats=True):
        for j in range(4):
            clear(ff.pad[:, j, 0:TAPS_FF - 1])
        f0 = 0
        for at, part in enumerate(PARTS):
            def body(i):
                for q in range(2):
                    f = 2 * i + q
                    for w in range(2):
                        j, b = 2 * q + w, 2 * (f0 + f) + w
                        e.wait_ge(c.evacuated, n.next(c.evacuated))
                        convolve(ff.conv[:, j, :], ff.pad[:, j, :], TAPS_FF, conv, b * TAPS_FF,
                                 col(c, bias, b) if bias else None)
                    e.wait_ge(c.silu_done, n.next(c.silu_done))
                    tt(ff.glu[:, q, :], ff.gate[:, q, :], ff.conv[:, 2 * q + 1, :], ALU.mult).then_inc(n.gave(c.glu_done), 1)
                    e.wait_ge(c.act_hi, n.next(c.act_hi))
                    tt(piece(ff.al, f), ff.glu[:, q, :], piece(ff.ah, f).bitcast(F32), ALU.subtract).then_inc(n.gave(c.act_ready), 1)
            n.repeat(part // 2, body)
            n.skip(c.block_done, 2 * part)
            residual(stats and at == len(PARTS) - 1)
            f0 += part

    if n.unsettled():
        e.wait_ge(n.last, n.now(n.last))
    e.memset(c.eps[:, :], EPS).then_inc(n.gave(c.eps_ready), 1)
    clear(c.acc[:, :])
    for k in range(DK):
        if k == 0:
            e.wait_ge(c.x_ready, n.next(c.x_ready, k=16 * DK // 2))
        tt(c.sq[:, k % 2, :], c.res[:, k, :], c.res[:, k, :], ALU.mult).then_inc(n.gave(c.vec_step), 1)
        tt(c.acc[:, :], c.acc[:, :], c.sq[:, k % 2, :], ALU.add).then_inc(n.gave(c.vec_step), 1)
    tell(c.sumsq_ready)
    e.wait_ge(c.cols_ready, n.next(c.cols_ready, k=16))
    norm_split("attn_norm")
    e.wait_ge(c.mix_ready, n.next(c.mix_ready, k=32))
    for s in range(2 * HEADS):
        x = (m1.rq if s < HEADS else m1.rk)[:, s % HEADS, :]
        e.wait_ge(c.evacuated, n.next(c.evacuated))
        tt(c.tmp[:, s % 3, :], x, m1.cos[:, :], ALU.mult).then_inc(n.gave(c.vec_step), 1)
        e.wait_ge(c.tile_for_vec, n.next(c.tile_for_vec))
        tt(c.sq[:, s % 2, :], bank[5 + s % 2][:, :], m1.sin[:, :], ALU.mult).then_inc(n.gave(c.vec_step), 1)
        tt(x, c.tmp[:, s % 3, :], c.sq[:, s % 2, :], ALU.add).then_inc(n.gave(c.vec_for_pe), 1)
    for at in range(HEADS * TB):
        h, w = at // TB, S - (at % TB) * P
        e.wait_ge(c.tile_for_vec, n.next(c.tile_for_vec))
        tt(m1.pt[:, at % 3, 0:w], bank[5 + at % 3][:, 0:w], m1.decay[:, h, 0:w], ALU.mult).then_inc(n.gave(c.vec_for_pe), 1)
    e.wait_ge(c.evacuated, n.next(c.evacuated, k=8))
    for h in range(HEADS):
        slice_scale(m1.mix[:, HEADS + h, :], None)
        tt(m1.mix[:, HEADS + h, :], m1.mix[:, HEADS + h, :], m1.rg[:, h, :], ALU.mult).then_inc(n.gave(c.vec_step), 1)
    for j in range(RING):
        clear(gd.pad[:, j, 0:TAPS_GDN - 1])
    clear(gd.rows[:, :])
    tell(c.vec_for_act)
    for b in range(12):
        e.wait_ge(c.evacuated, n.next(c.evacuated))
        y = (gd.q, gd.k, gd.v)[b // HEADS][:, b % HEADS, :]
        convolve(y, gd.pad[:, b % RING, :], TAPS_GDN, "gdn_conv", b * TAPS_GDN, None)
    e.wait_ge(c.act_for_vec, n.next(c.act_for_vec))
    tt(gd.wl[:, :, :], gd.w[:, :, :], gd.wh[:, :, :].bitcast(F32), ALU.subtract).then_inc(n.gave(c.small_split), 1)
    e.wait_ge(c.tile_for_vec, n.next(c.tile_for_vec))
    if n.unsettled():
        e.wait_ge(n.last, n.now(n.last))
    e.tensor_copy(gd.ab[:, :], bank[4][0:64, :]).then_inc(n.gave(c.vec_for_act), 1)
    z, az, ln = c.tmp[0:HEADS, 0, :], c.tmp[0:HEADS, 1, :], c.tmp[0:HEADS, 2, :]
    ts(z, gd.ab[0:HEADS, :], col(c, "dt_bias", parts=HEADS), None, ALU.add, None).then_inc(n.gave(c.vec_step), 1)
    ts(az, z, -1.0, None, ALU.mult, None).then_inc(n.gave(c.vec_step), 1)
    tt(az, z, az, ALU.max).then_inc(n.gave(c.vec_for_act), 1)
    if n.unsettled():
        e.wait_ge(n.last, n.now(n.last))
    e.memset(c.rs[:, :], 1.0).then_inc(n.gave(c.vec_step), 1)
    e.wait_ge(c.act_for_vec, n.next(c.act_for_vec))
    ts(z, z, 0.0, None, ALU.max, None).then_inc(n.gave(c.vec_step), 1)
    tt(z, z, ln, ALU.add).then_inc(n.gave(c.vec_step), 1)
    ts(az, z, gd.ea[0:HEADS, :], -1.0, ALU.mult, ALU.mult).then_inc(n.gave(c.vec_step), 1)
    for t in range(TB):
        cs = slice(t * P, (t + 1) * P)
        if n.unsettled():
            e.wait_ge(n.last, n.now(n.last))
        e.tensor_tensor_scan(gd.rows[0:HEADS, cs], c.rs[0:HEADS, 0:P], az[:, cs], 0.0, ALU.mult, ALU.add).then_inc(n.gave(c.vec_for_pe if t == TB - 1 else c.vec_step), 1)
    tell(c.vec_for_act)
    for h in range(HEADS):
        slice_scale(gd.q[:, h, :], float(P) ** -0.5)
    for h in range(HEADS):
        slice_scale(gd.k[:, h, :], None)
    tell(c.vec_for_pe)
    gc, beta = gd.cols[:, :, 0:HEADS], gd.cols[:, :, 32:32 + HEADS]
    last = gd.gr.rearrange("p h (t s) -> p t h s", s=P)[:, :, :, P - 1]
    e.wait_ge(c.act_for_vec, n.next(c.act_for_vec))
    tt(gd.kbgs[:, :, :], gd.egc[:, :, :], beta, ALU.mult).then_inc(n.gave(c.vec_step), 1)
    tt(gd.dl[:, :, :], last, gc, ALU.subtract).then_inc(n.gave(c.vec_for_act), 1)
    e.wait_ge(c.act_for_vec, n.next(c.act_for_vec))
    for t in range(TB):
        cs = slice(t * P, (t + 1) * P)
        d, above, below = (heads_view(c.tmp[:, i, :]) for i in range(3))
        tt(d, gd.gr[:, :, cs], over_columns(gc[:, t, :]), ALU.subtract).then_inc(n.gave(c.vec_step), 1)
        ts(above, d, 0.0, None, ALU.max, None).then_inc(n.gave(c.vec_step), 1)
        ts(below, d, 0.0, None, ALU.min, None).then_inc(n.gave(c.vec_for_act), 1)
        e.wait_ge(c.tile_for_vec, n.next(c.tile_for_vec))
        tt(heads_view(gd.kbg[:, :]), heads_view(bank[0][:, :]), over_columns(gd.kbgs[:, t, :]), ALU.mult).then_inc(n.gave(c.vec_step), 1)
        tt(heads_view(gd.kd[:, :]), heads_view(bank[0][:, :]), over_columns(gd.kds[:, t, :]), ALU.mult).then_inc(n.gave(c.vec_step), 1)
        e.wait_ge(c.tile_for_vec, n.next(c.tile_for_vec))
        tt(heads_view(gd.vb[:, :]), heads_view(bank[1][:, :]), over_columns(beta[:, t, :]), ALU.mult).then_inc(n.gave(c.vec_step), 1)
        e.wait_ge(c.act_for_vec, n.next(c.act_for_vec))
        dec = heads_view(gd.dec[:, 0, :])
        tt(dec, dec, over_heads(m1.lower[:, :]), ALU.mult).then_inc(n.gave(c.vec_step), 1)
        tt(dec, dec, over_columns(beta[:, t, :]), ALU.mult).then_inc(n.gave(c.vec_step), 1)
        e.wait_ge(c.tile_for_vec, n.next(c.tile_for_vec))
        tt(gd.M[:, :], bank[2][:, :], gd.dec[:, 0, :], ALU.mult).then_inc(n.gave(c.vec_step), 1)
        e.wait_ge(c.act_for_vec, n.next(c.act_for_vec))
        dec = heads_view(gd.dec[:, 1, :])
        tt(dec, dec, over_heads(m1.upper[:, :]), ALU.mult).then_inc(n.gave(c.vec_step), 1)
        e.wait_ge(c.tile_for_vec, n.next(c.tile_for_vec))
        tt(gd.qk[:, :], bank[3][:, :], gd.dec[:, 1, :], ALU.mult).then_inc(n.gave(c.vec_step), 1)
        e.wait_ge(c.act_for_vec, n.next(c.act_for_vec))
        tt(heads_view(gd.qd[:, :]), gd.q[:, :, cs], heads_view(gd.eg[:, :]), ALU.mult).then_inc(n.gave(c.vec_step), 1)

        def level(lv):
            return tt(heads_view(gd.lev[:, lv % 2, :]), heads_view(gd.M[:, :]),
               over_heads(m1.levels[:, lv * P:(lv + 1) * P]), ALU.mult)
        level(0).then_inc(n.gave(c.vec_step), 1)
        ident = over_heads(const(c, "ident"))
        tt(heads_view(gd.T[:, :]), ident, heads_view(gd.lev[:, 0, :]), ALU.subtract).then_inc(n.gave(c.vec_for_pe), 1)
        level(1).then_inc(n.gave(c.vec_step), 1)
        e.wait_ge(c.tile_for_vec, n.next(c.tile_for_vec))
        tt(heads_view(gd.U[:, :]), ident, heads_view(bank[4][:, :]), ALU.subtract).then_inc(n.gave(c.vec_for_pe), 1)
        for lv in range(1, LEVELS):
            if lv + 1 < LEVELS:
                level(lv + 1).then_inc(n.gave(c.vec_step), 1)
                e.wait_ge(c.tile_for_vec, n.next(c.tile_for_vec, k=2))
                tt(gd.T[:, :], gd.T[:, :], bank[5][:, :], ALU.subtract).then_inc(n.gave(c.vec_step), 1)
            else:
                e.wait_ge(c.tile_for_vec, n.next(c.tile_for_vec))
            tt(gd.U[:, :], gd.U[:, :], bank[6][:, :], ALU.subtract).then_inc(n.gave(c.vec_for_pe), 1)
        if t < TB - 1:
            e.wait_ge(c.tile_for_vec, n.next(c.tile_for_vec))
            if t == 0:
                if n.unsettled():
                    e.wait_ge(n.last, n.now(n.last))
                e.tensor_copy(gd.state[:, :], bank[2][:, :]).then_inc(n.gave(c.vec_for_pe), 1)
            else:
                tt(heads_view(gd.state[:, :]), heads_view(gd.state[:, :]), over_columns(gd.cd[:, t, :]), ALU.mult).then_inc(n.gave(c.vec_step), 1)
                tt(gd.state[:, :], gd.state[:, :], bank[2][:, :], ALU.add).then_inc(n.gave(c.vec_for_pe), 1)
    e.wait_ge(c.evacuated, n.next(c.evacuated, k=4))
    for h in range(HEADS):
        slice_scale(m1.mix[:, h, :], col(c, "gdn_norm"))
        tt(m1.mix[:, h, :], m1.mix[:, h, :], gd.gr[:, h, :], ALU.mult).then_inc(n.gave(c.vec_step), 1)
    tell(c.vec_for_act)
    low_parts(m1.mix)
    n.skip(c.block_done, 32)
    residual()
    norm_split("mlp_norm")
    feed_forward("mlp_conv", None)
    e.wait_ge(c.root_done, n.next(c.root_done))
    clear(c.acc[:, :])
    for k in range(DK + 1):
        if k < DK:
            x = c.res[:, k, :]
            stt(x, x, col(c, "final_norm", k), c.root[:, :], ALU.mult, ALU.mult).then_inc(n.gave(c.vec_for_act), 1)
        if k >= 1:
            e.wait_ge(c.act_for_vec, n.next(c.act_for_vec))
            tt(c.acc[:, :], c.acc[:, :], c.sq[:, (k - 1) % 2, :], ALU.add).then_inc(n.gave(c.vec_step), 1)
    tell(c.sumsq_ready)
    norm_split("even_norm")
    for g in range(len(WINDOWS)):
        clear(m2.pool[:, g, 0:16])
    e.wait_ge(c.act_for_vec, n.next(c.act_for_vec))
    tt(m2.wl[:, :, :], m2.w[:, :, :], m2.wh[:, :, :].bitcast(F32), ALU.subtract).then_inc(n.gave(c.small_split), 1)
    ts(m2.qs[:, :], col(c, "q_norm"), float(AD) ** -0.5, None, ALU.mult, None).then_inc(n.gave(c.vec_step), 1)
    z, az, ln = c.tmp[0:AH, 0, :], c.tmp[0:AH, 1, :], c.tmp[0:AH, 2, :]
    e.wait_ge(c.tile_for_vec, n.next(c.tile_for_vec))
    ts(z, bank[4][0:AH, :], col(c, "b_f", parts=AH), None, ALU.add, None).then_inc(n.gave(c.vec_step), 1)
    ts(az, z, -1.0, None, ALU.mult, None).then_inc(n.gave(c.vec_step), 1)
    tt(az, z, az, ALU.max).then_inc(n.gave(c.vec_for_act), 1)
    if n.unsettled():
        e.wait_ge(n.last, n.now(n.last))
    e.memset(c.rs[:, :], 1.0).then_inc(n.gave(c.vec_step), 1)
    e.wait_ge(c.act_for_vec, n.next(c.act_for_vec))
    ts(z, z, 0.0, None, ALU.min, None).then_inc(n.gave(c.vec_step), 1)
    tt(z, z, ln, ALU.subtract).then_inc(n.gave(c.vec_step), 1)
    if n.unsettled():
        e.wait_ge(n.last, n.now(n.last))
    e.tensor_tensor_scan(m2.rows[:, :], c.rs[0:AH, :], z, 0.0, ALU.mult, ALU.add).then_inc(n.gave(c.vec_for_pe), 1)
    tell(c.vec_for_act)
    for h in range(HEADS):
        slice_scale(m2.q[:, h, :], m2.qs[:, 0:1])
    for h in range(HEADS):
        slice_scale(m2.k[:, h, :], col(c, "k_norm"))
    tell(c.vec_for_pe)

    def softmax(at):
        h, t = at // TB, at % TB
        w, s = (t + 1) * P, m2.s[:, at % 3, :]
        if t == 0:
            e.wait_ge(c.row_ready, n.next(c.row_ready))
        e.wait_ge(c.tile_for_vec, n.next(c.tile_for_vec))
        stt(s[:, 0:w], bank[SCORE_BANKS[at % 3]][:, 0:w], m2.ccol[:, t * AH + h:t * AH + h + 1], m2.nrow[:, h % 2, 0:w],
            ALU.add, ALU.add).then_inc(n.gave(c.vec_step), 1)
        tt(s[:, t * P:w], s[:, t * P:w], const(c, "causal"), ALU.add).then_inc(n.gave(c.vec_step), 1)
        if n.unsettled():
            e.wait_ge(n.last, n.now(n.last))
        e.tensor_reduce(m2.nmax[:, at % 3:at % 3 + 1], s[:, 0:w], AX, ALU.max, negate=True).then_inc(n.gave(c.vec_for_act), 1)

    softmax(0)
    softmax(1)
    for at in range(AH * TB):
        w = (at % TB + 1) * P
        e.wait_ge(c.act_for_vec, n.next(c.act_for_vec))
        if n.unsettled():
            e.wait_ge(n.last, n.now(n.last))
        e.reciprocal(m2.rsum[:, 0:1], m2.sum[:, at % 3:at % 3 + 1]).then_inc(n.gave(c.vec_step), 1)
        ts(m2.p[:, at % 3, 0:w], m2.p[:, at % 3, 0:w], m2.rsum[:, 0:1], None, ALU.mult, None).then_inc(n.gave(c.vec_for_pe), 1)
        if at + 2 < AH * TB:
            softmax(at + 2)
    e.wait_ge(c.evacuated, n.next(c.evacuated, k=16))
    for g, window in enumerate(WINDOWS):
        x, width = m2.pool[:, g, :], 1
        while width < window:
            y = m2.win[:, 0 if width in (1, 4) else 1, :]
            tt(y[:, 2 * width - 1:], x[:, 2 * width - 1:], x[:, width - 1:16 + S - width], ALU.add).then_inc(n.gave(c.vec_step), 1)
            x, width = y, 2 * width
        u, out = m2.pool[:, g, 16:], m2.q[:, g, :]
        stt(out, x[:, 16:], 1.0 / window, u, ALU.mult, ALU.subtract).then_inc(n.gave(c.vec_step), 1)
        tt(out[:, 0:16], x[:, 16:32], const(c, "count")[:, g * 16:(g + 1) * 16], ALU.mult).then_inc(n.gave(c.vec_step), 1)
        tt(out[:, 0:16], out[:, 0:16], u[:, 0:16], ALU.subtract).then_inc(n.gave(c.vec_for_pe), 1)
    low_parts(m2.mix)
    n.skip(c.block_done, 16)
    residual()
    norm_split("ffn_norm0")
    feed_forward("ffn_conv0", "ffn_bias0")
    norm_split("odd_norm")
    clear(cf.pad[:, 0, 0:TAPS_DW - 1])
    clear(cf.pad[:, 1, 0:TAPS_DW - 1])
    clear(c.acc[:, :])
    e.wait_ge(c.act_for_vec, n.next(c.act_for_vec))
    tt(cf.dw_l[:, :], c.cols[:, COL_AT["dw"]:COL_AT["dw"] + DK * TAPS_DW], cf.dw_h[:, :].bitcast(F32),
       ALU.subtract).then_inc(n.gave(c.vec_for_act), 1)

    def depthwise(i):
        def gated(q):
            e.wait_ge(c.evacuated, n.next(c.evacuated, k=2))
            tt(cf.pad[:, q, TAPS_DW - 1:], cf.val[:, q, :], cf.gate[:, q, :], ALU.mult).then_inc(n.gave(c.glu_done), 1)

        def low(q):
            e.wait_ge(c.pad_hi, n.next(c.pad_hi))
            tt(cf.pad_l[:, q, :], cf.pad[:, q, :], cf.pad_h[:, q, :].bitcast(F32), ALU.subtract).then_inc(n.gave(c.pad_ready), 1)

        def taps(q, rounds):
            for r in rounds:
                for which, y in enumerate((cf.y[:, q, :], cf.z[:, q, :])):
                    tap = TAPS_DW - 1 - 2 * r - which
                    if tap < PE_TAPS:
                        continue
                    if which == 0 and n.unsettled():
                        e.wait_ge(n.last, n.now(n.last))
                    x, w = cf.pad[:, q, tap:tap + S], cf.tap[:, q * TAPS_DW + tap:q * TAPS_DW + tap + 1]
                    if r == 0:
                        bias = col(c, "dw_b", 2 * i + q) if which == 0 else 0.0
                        e.tensor_scalar(y, x, w, bias, ALU.mult, ALU.add).then_inc(n.gave(c.vec_step), 1)
                    else:
                        e.scalar_tensor_tensor(out=y, in0=x, scalar=w, in1=y, op0=ALU.mult,
                                               op1=ALU.add).then_inc(n.gave(c.vec_step), 1)

        rounds = (TAPS_DW - PE_TAPS + 1) // 2
        ts(cf.tap[:, :], c.cols[:, bass.ds(COL_AT["dw"] + 2 * i * TAPS_DW, 2 * TAPS_DW)], 1.0, None,
           ALU.mult, None).then_inc(n.gave(c.vec_step), 1)
        gated(0)
        taps(0, range(7))
        gated(1)
        low(0)
        taps(0, range(7, rounds))
        taps(1, range(2))
        low(1)
        taps(1, range(2, rounds))
        for q in range(2):
            y = piece(cf.u, 2 * i + q)
            e.wait_ge(c.taps_done, n.next(c.taps_done))
            tt(cf.z[:, q, :], cf.z[:, q, :], bank[5 + q][:, :], ALU.add).then_inc(n.gave(c.taps_used), 1)
            tt(y, cf.y[:, q, :], cf.z[:, q, :], ALU.add).then_inc(n.gave(c.vec_step), 1)
            tt(c.acc[:, :], c.acc[:, :], y, ALU.add).then_inc(n.gave(c.vec_step), 1)
    n.repeat(DK // 2, depthwise)
    n.skip(c.block_done, 16)
    tell(c.sumsq_ready)
    e.wait_ge(c.root_done, n.next(c.root_done))
    clear(c.acc[:, :])
    for k in range(DK + 1):
        if k < DK:
            tt(cf.u[:, k, :], cf.u[:, k, :], c.root[:, :], ALU.subtract).then_inc(n.gave(c.vec_for_act), 1)
        if k >= 1:
            e.wait_ge(c.act_for_vec, n.next(c.act_for_vec))
            tt(c.acc[:, :], c.acc[:, :], c.sq[:, (k - 1) % 2, :], ALU.add).then_inc(n.gave(c.vec_step), 1)
    tell(c.sumsq_ready)
    e.wait_ge(c.root_done, n.next(c.root_done))
    for k in range(DK + 1):
        if k < DK:
            tt(c.tmp[:, k % 3, :], cf.u[:, k, :], c.root[:, :], ALU.mult).then_inc(n.gave(c.norm_tmp), 1)
        if k >= 1:
            e.wait_ge(c.norm_hi, n.next(c.norm_hi))
            tt(c.nl[:, k - 1, :], cf.y[:, (k - 1) % 2, :], c.nh[:, k - 1, :].bitcast(F32), ALU.subtract).then_inc(n.gave(c.norm_ready), 1)
    residual()
    norm_split("ffn_norm1")
    feed_forward("ffn_conv1", "ffn_bias1", stats=False)



def pool_program(c, e):
    n = Counts(e)

    def body(i):
        for j in range(RING):
            e.wait_ge(c.hi_ready, n.next(c.hi_ready))
            e.tensor_tensor(c.wl[:, j, :], c.raw[:, j, :], c.wh[:, j, :].bitcast(F32), ALU.subtract).then_inc(n.gave(c.lo_ready), 1)
    n.repeat(NBLOCKS // RING, body)



def sync_program(c, m1, gd, m2, d, out, e):
    n = Counts(e)

    def blocks(w, width=BLK):
        def body(i):
            for j in range(RING):
                if n.passed(c.lo_ready, lag=RING):
                    e.wait_ge(c.lo_ready, n.now(c.lo_ready, lag=RING))
                b = RING * i + j
                src = w[b] if type(b) is int else w[bass.ds(b, 1)].rearrange("a p n -> (a p) n")
                e.dma_start(c.raw[:, j, 0:width], src).then_inc(c.raw_ready[j], 16)
        n.repeat(w.shape[0] // RING, body)

    def feed_forward(f):
        for at in range(len(PARTS)):
            blocks(d[f"{f}_up{at}"])
            blocks(d[f"{f}_down{at}"], PARTS[at] * P)

    for k in range(0, DK, 2):
        e.dma_start(c.res[:, k:k + 2, :], d["x"][:, k:k + 2, :]).then_inc(c.x_ready, 16)
    e.dma_start(c.consts[:, :], d["consts"]).then_inc(c.consts_ready, 16)
    e.dma_start(c.cols[:, :], d["cols"]).then_inc(c.cols_ready, 16)
    e.dma_start(m1.consts[:, :], d["mix_consts"]).then_inc(c.mix_ready, 16)
    e.dma_start(m1.ret_consts[:, :], d["ret_consts"]).then_inc(c.mix_ready, 16)
    blocks(d["w_in"][0:16])
    blocks(d["w_in"][16:24])
    e.wait_ge(c.conv_done, 1)
    e.dma_start(gd.w[:, :, :], d["ab"]).then_inc(c.small_ready, 16)
    blocks(d["w_in"][24:32])
    blocks(d["w_out"])
    feed_forward("ff_a")
    blocks(d["even_in"][0:8])
    e.wait_ge(c.added, (1 + len(PARTS)) * DK)
    e.dma_start(m2.w[:, :, :], d["f"]).then_inc(c.small_ready, 16)
    e.dma_start(m2.wpool[:, :, :], d["wpool"]).then_inc(c.small_ready, 16)
    blocks(d["even_in"][8:16])
    blocks(d["even_out"])
    feed_forward("ff_b")
    blocks(d["pw1"])
    blocks(d["pw2"])
    feed_forward("ff_c")
    e.wait_ge(c.added, (3 + 3 * len(PARTS)) * DK)
    for k in range(0, DK, 2):
        e.dma_start(out[:, k:k + 2, :], c.res[:, k:k + 2, :]).then_inc(c.out_stored, 16)
    e.wait_ge(c.out_stored, 16 * DK // 2)


def build(nc, d, out):
    with ExitStack() as ctx:
        c = allocate(nc, ctx)

        def region(stack, phase, **spec):
            return {name: stack.enter_context(nc.sbuf_tensor(f"{phase}_{name}", shape, dt))
                    for name, (shape, dt) in spec.items()}

        with ExitStack() as mix:
            shared = region(mix, "mixer1", mix=([P, 2 * HEADS, S], F32), consts=([P, sum(MIX_CONSTS.values())], F32))
            at = 0
            for name, w in MIX_CONSTS.items():
                shared[name] = shared["consts"][:, at:at + w]
                at += w
            with ExitStack() as ret:
                own = region(ret, "retention", ret_consts=([P, sum(RET_CONSTS.values())], F32),
                             rq=([P, HEADS, S], F32), rk=([P, HEADS, S], F32), rv=([P, TB, S], F32),
                             rg=([P, HEADS, S], F32), pt=([P, 3, S], F32))
                tables = own["ret_consts"]
                m1 = names(cos=tables[:, 0:S], sin=tables[:, S:2 * S],
                                     decay=tables[:, 2 * S:].rearrange("p (h s) -> p h s", h=HEADS), **shared, **own)
            with ExitStack() as net:
                own = region(net, "gdn", q=([P, HEADS, S], F32), k=([P, HEADS, S], F32), v=([P, HEADS, S], F32),
                             rows=([64, S], F32), ea=([P, 1], F32), cols=([P, TB, 64], F32),
                             gr=([P, HEADS, S], F32), egc=([P, TB, HEADS], F32), cd=([P, TB, HEADS], F32),
                             kbgs=([P, TB, HEADS], F32), kds=([P, TB, HEADS], F32), dl=([P, TB, HEADS], F32))
                with ExitStack() as early:
                    own |= region(early, "gdn", pad=([P, RING, TAPS_GDN - 1 + S], F32), w=([P, DK, P], F32),
                                  wh=([P, DK, P], F32R), wl=([P, DK, P], F32R), ab=([64, S], F32))
                own |= region(net, "gdn", dec=([P, 2, S], F32), **{
                    name: ([P, S], F32) for name in "eg kbg kd vb M qk qd T U nw u state".split()})
                gd = names(lev=c.sq, Z=c.root, **own)
        with ExitStack() as feed:
            ff = names(**region(
                feed, "ff", ah=([P, max(PARTS), S], F32R), al=([P, max(PARTS), S], F32R),
                pad=([P, 4, TAPS_FF - 1 + S], F32), conv=([P, 4, S], F32), gate=([P, 2, S], F32),
                glu=([P, 2, S], F32)))
        with ExitStack() as att:
            own = region(att, "att", q=([P, HEADS, S], F32), k=([P, HEADS, S], F32), v=([P, TB, S], F32),
                         pool=([P, len(WINDOWS), 16 + S], F32), mix=([P, 2 * HEADS, S], F32), rows=([AH, S], F32),
                         qs=([P, 1], F32), ccol=([P, TB * AH], F32), nrow=([P, 2, S], F32), nmax=([P, 3], F32),
                         sum=([P, 3], F32), rsum=([P, 1], F32), wpool=([P, len(WINDOWS), P], F32))
            with ExitStack() as early:
                own |= region(early, "att", w=([P, DK, P], F32), wh=([P, DK, P], F32R), wl=([P, DK, P], F32R))
            own |= region(att, "att", s=([P, 3, S], F32), p=([P, 3, S], F32), pt=([P, 2, S], F32),
                          win=([P, 2, 16 + S], F32))
            m2 = names(**own)
        with ExitStack() as con:
            cf = names(**region(
                con, "conf", val=([P, 2, S], F32), gate=([P, 2, S], F32), pad=([P, 2, TAPS_DW - 1 + S], F32),
                u=([P, DK, S], F32), y=([P, 2, S], F32), z=([P, 2, S], F32),
                pad_h=([P, 2, TAPS_DW - 1 + S], F32R), pad_l=([P, 2, TAPS_DW - 1 + S], F32R),
                diag_h=([P, 2, PE_TAPS, P], F32R), diag_l=([P, 2, PE_TAPS, P], F32R),
                tap=([P, 2 * TAPS_DW], F32), tap_h=([P, 2 * TAPS_DW], F32), tap_l=([P, 2 * TAPS_DW], F32),
                dw_h=([P, DK * TAPS_DW], F32R), dw_l=([P, DK * TAPS_DW], F32)))

        block = ctx.enter_context(nc.Block())

        @block.tensor
        def _(e):
            tensor_program(c, m1, gd, ff, m2, cf, e)

        @block.scalar
        def _(e):
            scalar_program(c, m1, gd, ff, m2, cf, e)

        @block.vector
        def _(e):
            vector_program(c, m1, gd, ff, m2, cf, e)

        @block.gpsimd
        def _(e):
            pool_program(c, e)

        @block.sync
        def _(e):
            sync_program(c, m1, gd, m2, d, out, e)



def shape_constants():
    i = np.arange(P)
    out = dict(ones=np.ones((P, P)), ident=np.eye(P))
    out["half_ones"] = (i[:, None] // AD == i[None, :] // AD) * 1.0
    out["causal"] = np.where(i[None, :] <= i[:, None], 0.0, NEG)
    out["select"] = np.concatenate([np.repeat((i == h)[:, None] * 1.0, P, 1) for h in range(AH)], 1)
    t = np.arange(16)
    out["count"] = np.concatenate([np.repeat((1.0 / np.minimum(t + 1, w))[None], P, 0) for w in WINDOWS], 1)
    rotate = np.zeros((P, P))
    rotate[i[1::2], i[0::2]] = -1.0
    rotate[i[0::2], i[1::2]] = 1.0
    out["rotate"] = rotate
    out["lower"] = (i[None, :] < i[:, None]) * 1.0
    out["upper"] = (i[None, :] >= i[:, None]) * 1.0
    levels = []
    for lv in range(LEVELS):
        a, b = i[:, None] >> lv, i[None, :] >> lv
        levels.append(((a >> 1) == (b >> 1)) * (a == b + 1) * 1.0)
    out["levels"] = np.concatenate(levels, 1)
    angle = 1.0 / (10000.0 ** np.linspace(0.0, 1.0, P // 2, dtype=np.float32).astype(np.float64))
    phase = (np.arange(S, dtype=np.float32)[None, :] * np.repeat(angle, 2).astype(np.float32)[:, None])
    out["cos"], out["sin"] = np.cos(phase.astype(np.float64)), np.sin(phase.astype(np.float64))
    rel = np.arange(S)[None, :] - i[:, None]
    decay = [np.where(rel >= 0, np.exp(rel * np.log(1.0 - 2.0 ** (-5.0 - h))), 0.0) * P ** -0.5 for h in range(HEADS)]
    out["decay"] = np.concatenate(decay, 1)
    pack = lambda names: np.ascontiguousarray(np.concatenate([out[m] for m in names], 1).astype(np.float32))
    return pack(CONSTS), pack(MIX_CONSTS), pack(RET_CONSTS)


def lay_out(a):
    def blocks(w, order=None):
        k, m = w.shape[0] // P, w.shape[1] // P
        t = w.reshape(k, P, m, P).transpose(2, 1, 0, 3)
        return np.ascontiguousarray((t if order is None else t[order]).reshape(-1, P, k * P))

    def token_blocks(w):
        return np.ascontiguousarray(w.reshape(4, 2, P, S).transpose(0, 2, 1, 3).reshape(4, P, 2 * S))

    def narrow(parts):
        w = np.zeros((D, P), np.float32)
        for at, v in parts:
            w[:, at:at + v.shape[1]] = v
        return np.ascontiguousarray(w.reshape(DK, P, P).transpose(1, 0, 2))

    def vector(v):
        return v.reshape(-1, P).T

    def taps(w, order=None):
        t = w.reshape(w.shape[0], -1, P).transpose(2, 1, 0)
        return (t if order is None else t[:, order]).reshape(P, -1)

    def padded(v):
        out = np.zeros((P, 1), np.float32)
        out[:v.shape[0], 0] = v
        return out

    w = a["w_in"][0]
    g = S
    gq, gk, gv, gg = (w[:, i * g:(i + 1) * g] for i in range(4))
    ab = w[:, 4 * g:4 * g + 2 * HEADS]
    rq, rk, rv, rg = (w[:, 4 * g + 2 * HEADS + i * g:4 * g + 2 * HEADS + (i + 1) * g] for i in range(4))
    d = dict(x=np.ascontiguousarray(a["x"][0].T.reshape(DK, P, S).transpose(1, 0, 2)))
    d["w_in"] = np.concatenate([blocks(rq), blocks(rk), token_blocks(rv), blocks(rg), blocks(gq), blocks(gk),
                                blocks(gv), blocks(gg)])
    d["ab"] = narrow([(0, ab[:, :HEADS]), (32, ab[:, HEADS:])])
    d["w_out"] = blocks(a["w_out"][0])
    pairs = np.arange(2 * FC).reshape(2, FC).T.reshape(-1)
    for name, up, down in (("ff_a", a["w_up"][0], a["w_down"][0]),
                           ("ff_b", a["ffn_w_up_2"][0], a["ffn_w_down_2"][0]),
                           ("ff_c", a["ffn_w_up_2"][1], a["ffn_w_down_2"][1])):
        f = 0
        for at, part in enumerate(PARTS):
            d[f"{name}_up{at}"] = blocks(up, pairs[2 * f:2 * (f + part)])
            d[f"{name}_down{at}"] = blocks(down[f * P:(f + part) * P])
            f += part
    w = a["even_w_in_2"][0]
    q, k, v, u = (w[:, i:i + S] for i in (0, S, 2 * S, 3 * S + AH))
    d["even_in"] = np.concatenate([blocks(q), blocks(k), token_blocks(v), blocks(u)])
    d["f"] = narrow([(0, w[:, 3 * S:3 * S + AH])])
    d["wpool"] = np.ascontiguousarray(a["even_w_pool_2"][0].transpose(1, 0, 2))
    d["even_out"] = blocks(a["even_w_out_2"][0])
    d["pw1"] = blocks(a["odd_w_pw1_2"][0], np.arange(2 * DK).reshape(2, DK).T.reshape(-1))
    d["pw2"] = blocks(a["odd_w_pw2_2"][0])
    twice = lambda v: np.concatenate([v, v])[:, None]
    cols = dict(attn_norm=vector(a["attn_norm_w"][0]), mlp_norm=vector(a["mlp_norm_w"][0]),
                final_norm=vector(a["final_norm_w"]), even_norm=vector(a["even_norm_g_2"][0]),
                odd_norm=vector(a["odd_norm_g_2"][0]), ffn_norm0=vector(a["ffn_norm_g_2"][0]),
                ffn_norm1=vector(a["ffn_norm_g_2"][1]), ln_g=vector(a["odd_ln_g_2"][0]),
                ln_b=vector(a["odd_ln_b_2"][0]), dw_b=vector(a["odd_dw_b_2"][0]),
                pool_scale=vector(a["even_pool_scale_2"][0]), gdn_norm=vector(a["gdn_norm_w"][0]),
                q_norm=twice(a["even_q_norm_g_2"][0]), k_norm=twice(a["even_k_norm_g_2"][0]),
                a_log=padded(a["gdn_a_log"][0]), dt_bias=padded(a["gdn_dt_bias"][0]),
                b_f=padded(a["even_b_f_2"][0]), gdn_conv=taps(a["gdn_conv_w"][0]),
                mlp_conv=taps(a["mlp_conv_w"][0], pairs), ffn_conv0=taps(a["ffn_conv_w_2"][0], pairs),
                ffn_conv1=taps(a["ffn_conv_w_2"][1], pairs), ffn_bias0=vector(a["ffn_conv_b_2"][0])[:, pairs],
                ffn_bias1=vector(a["ffn_conv_b_2"][1])[:, pairs], dw=taps(a["odd_dw_w_2"][0]))
    d["cols"] = np.ascontiguousarray(np.concatenate([cols[m] for m in COLS], 1))
    d["consts"], d["mix_consts"], d["ret_consts"] = shape_constants()
    return d


def kernel(**inputs):
    import concourse.bacc as bacc
    from concourse.bass_utils import run_bass_kernel_spmd

    nc = bacc.Bacc("TRN2", target_bir_lowering=False, num_devices=1)
    arrays, d = {}, {}
    for name, a in lay_out({k: np.asarray(v) for k, v in inputs.items()}).items():
        arrays[f"in_{name}"] = a
        d[name] = nc.dram_tensor(f"in_{name}", a.shape, mybir.dt.from_np(a.dtype), kind="ExternalInput").ap()
    out = nc.dram_tensor("out", (P, DK, S), F32, kind="ExternalOutput").ap()
    build(nc, d, out)
    r = run_bass_kernel_spmd(nc, [arrays], core_ids=[0])
    got = np.asarray(r.results[0]["out"])
    return np.ascontiguousarray(got.transpose(1, 0, 2).reshape(D, S).T)[None]
```
